# Optimizing a Trainium2 kernel written in Bass

```python
import math
import jax, jax.numpy as jnp
from jax import lax
import numpy as np

D_MODEL = 1024
BATCH = 1
SEQ = 1024
DEPTH = 1

CHUNK = 64
D_MIX = D_MODEL
SB_HEADS = 8
SB_HEAD_DIM = 64
D_SB = SB_HEADS * SB_HEAD_DIM
CONV_GROUPS = 8
D_CONV = D_MIX - D_SB
CONV_WIDTH = 3
Q_BLOCK = 128
D_IN_PROJ = 3 * D_SB + 3 * D_CONV
PEER_HEADS = 8
N_KEYS = 128
N_EXPERTS = N_KEYS * N_KEYS
D_KEY = 256
D_HALF = D_KEY // 2
TOPK_HALF = 16
TOPK = 16
TOKEN_BLOCK = 128
EPS = 1e-6

kernel_name = "hymba_stickbreak_shortconv_peer_block"

def _rmsnorm(x, g):
    x32 = x.astype(jnp.float32)
    inv = lax.rsqrt(jnp.mean(x32 * x32, axis=-1, keepdims=True) + EPS)
    return (x32 * inv).astype(x.dtype) * g

def _stick_breaking(q, k, v):
    seq = q.shape[2]
    scale = 1.0 / math.sqrt(q.shape[-1])
    outs = []
    for i in range(seq // Q_BLOCK):
        q0 = i * Q_BLOCK
        kv_len = q0 + Q_BLOCK
        qb = q[:, :, q0:kv_len].astype(jnp.float32)
        kb = k[:, :, :kv_len].astype(jnp.float32)
        vb = v[:, :, :kv_len]
        z = jnp.einsum('bhqd,bhkd->bhqk', qb, kb) * scale
        t_pos = q0 + jnp.arange(Q_BLOCK)
        s_pos = jnp.arange(kv_len)
        mask = s_pos[None, :] < t_pos[:, None]
        log_beta = jax.nn.log_sigmoid(z)
        log_1m = jnp.where(mask, jax.nn.log_sigmoid(-z), 0.0)
        log_stick = lax.cumsum(log_1m, axis=3, reverse=True) - log_1m
        a = jnp.where(mask, jnp.exp(log_beta + log_stick), 0.0)
        outs.append(jnp.einsum('bhqk,bhkd->bhqd', a.astype(vb.dtype), vb))
    return jnp.concatenate(outs, axis=2)

def _short_conv(xc, b_gate, c_gate, conv_w):
    seq = xc.shape[1]
    u = c_gate * xc
    up = jnp.pad(u, ((0, 0), (CONV_WIDTH - 1, 0), (0, 0)))
    y = sum(conv_w[w] * up[:, w:w + seq] for w in range(CONV_WIDTH))
    return b_gate * y

def _peer(h, w_q, sub_keys, expert_u, expert_v):
    bsz, seq, d = h.shape
    tok = h.reshape(bsz * seq, d)
    q = (tok @ w_q).reshape(-1, PEER_HEADS, D_KEY)
    q1, q2 = q[..., :D_HALF], q[..., D_HALF:]
    s1 = jnp.einsum('thd,kd->thk', q1, sub_keys[0]).astype(jnp.float32)
    s2 = jnp.einsum('thd,kd->thk', q2, sub_keys[1]).astype(jnp.float32)
    v1, i1 = lax.top_k(s1, TOPK_HALF)
    v2, i2 = lax.top_k(s2, TOPK_HALF)
    cand_s = (v1[..., :, None] + v2[..., None, :]).reshape(-1, PEER_HEADS, TOPK_HALF * TOPK_HALF)
    cand_i = (i1[..., :, None] * N_KEYS + i2[..., None, :]).reshape(-1, PEER_HEADS, TOPK_HALF * TOPK_HALF)
    top_s, pos = lax.top_k(cand_s, TOPK)
    idx = jnp.take_along_axis(cand_i, pos, axis=-1)
    gate = jax.nn.softmax(top_s, axis=-1).astype(h.dtype)

    n_blk = tok.shape[0] // TOKEN_BLOCK
    xb = tok.reshape(n_blk, TOKEN_BLOCK, d)
    ib = idx.reshape(n_blk, TOKEN_BLOCK, PEER_HEADS, TOPK)
    gb = gate.reshape(n_blk, TOKEN_BLOCK, PEER_HEADS, TOPK)

    def block_fn(args):
        xt, it, gt = args
        u = expert_u[it]
        vv = expert_v[it]
        act = jax.nn.gelu(jnp.einsum('thkd,td->thk', u, xt), approximate=False)
        return jnp.einsum('thk,thkd->td', gt * act, vv)

    out = lax.map(block_fn, (xb, ib, gb))
    return out.reshape(bsz, seq, d)

def setup_inputs(seed: int = 0) -> dict:
    key = jax.random.key(seed)
    ks = jax.random.split(key, 16)
    f32 = jnp.float32

    def gain(k, n):
        return (1.0 + 0.02 * jax.random.normal(k, (DEPTH, n))).astype(f32)

    return {
        "x": jax.random.normal(ks[0], (BATCH, SEQ, D_MODEL), f32),
        "norm1_g": gain(ks[1], D_MODEL),
        "w_in": jax.random.normal(ks[2], (DEPTH, D_MODEL, D_IN_PROJ), f32) * D_MODEL ** -0.5,
        "q_norm_g": gain(ks[3], SB_HEAD_DIM),
        "k_norm_g": gain(ks[4], SB_HEAD_DIM),
        "conv_w": jax.random.normal(ks[5], (DEPTH, CONV_WIDTH, D_CONV), f32) * CONV_WIDTH ** -0.5,
        "sb_out_g": gain(ks[6], D_SB),
        "conv_out_g": gain(ks[7], D_CONV),
        "w_out": jax.random.normal(ks[8], (DEPTH, D_MIX, D_MODEL), f32) * D_MIX ** -0.5,
        "norm2_g": gain(ks[9], D_MODEL),
        "peer_w_q": jax.random.normal(ks[10], (DEPTH, D_MODEL, PEER_HEADS * D_KEY), f32) * D_MODEL ** -0.5,
        "peer_sub_keys": jax.random.normal(ks[11], (DEPTH, 2, N_KEYS, D_HALF), f32) * D_HALF ** -0.5,
        "peer_u": jax.random.normal(ks[12], (DEPTH, N_EXPERTS, D_MODEL), f32) * D_MODEL ** -0.5,
        "peer_v": jax.random.normal(ks[13], (DEPTH, N_EXPERTS, D_MODEL), f32) * 0.5,
    }

def reference(x, norm1_g, w_in, q_norm_g, k_norm_g, conv_w, sb_out_g, conv_out_g,
              w_out, norm2_g, peer_w_q, peer_sub_keys, peer_u, peer_v):
    bsz, seq, _ = x.shape
    for l in range(DEPTH):
        h = _rmsnorm(x, norm1_g[l])
        proj = h @ w_in[l]
        q, k, v, xc, b_gate, c_gate = jnp.split(
            proj, [D_SB, 2 * D_SB, 3 * D_SB, 3 * D_SB + D_CONV, 3 * D_SB + 2 * D_CONV], axis=-1)
        q = _rmsnorm(q.reshape(bsz, seq, SB_HEADS, SB_HEAD_DIM), q_norm_g[l]).transpose(0, 2, 1, 3)
        k = _rmsnorm(k.reshape(bsz, seq, SB_HEADS, SB_HEAD_DIM), k_norm_g[l]).transpose(0, 2, 1, 3)
        v = v.reshape(bsz, seq, SB_HEADS, SB_HEAD_DIM).transpose(0, 2, 1, 3)
        sb = _stick_breaking(q, k, v).transpose(0, 2, 1, 3).reshape(bsz, seq, D_SB)
        cv = _short_conv(xc, b_gate, c_gate, conv_w[l])
        mixed = jnp.concatenate([_rmsnorm(sb, sb_out_g[l]), _rmsnorm(cv, conv_out_g[l])], axis=-1)
        x = x + mixed @ w_out[l]
        h2 = _rmsnorm(x, norm2_g[l])
        x = x + _peer(h2, peer_w_q[l], peer_sub_keys[l], peer_u[l], peer_v[l])
    return x


_drawn_inputs = setup_inputs


def setup_inputs(seed=0):
    import zlib

    import numpy as np

    out = dict(_drawn_inputs(seed))
    spreads = {}
    factors = {'q_norm_g': 11.161,
     'k_norm_g': 15.521,
     'conv_out_g': 2.81,
     'sb_out_g': 5.178,
     'norm2_g': 3.55}
    for name, (base, spread) in spreads.items():
        noise = np.random.default_rng([zlib.crc32(name.encode()), seed]).standard_normal(out[name].shape)
        drawn = base * np.exp(spread * noise) if base else spread * noise
        out[name] = __import__('jax').numpy.asarray(drawn.astype(out[name].dtype))
    for name, factor in factors.items():
        out[name] = (out[name] * factor).astype(out[name].dtype)
    return out
```

```python
from contextlib import ExitStack

import concourse.bass as bass
from concourse import mybir

F32 = mybir.dt.float32
BF16 = mybir.dt.bfloat16
U32 = mybir.dt.uint32
I32 = mybir.dt.int32
ALU = mybir.AluOpType
ACT = mybir.ActivationFunctionType
AX_X = mybir.AxisListType.X

P = 128
D = 1024
S = 1024
BLOCKS = S // P
KD = D // P
HEADS = 8
DH = 64
DSB = HEADS * DH
CH = DSB // P
SCALE = DH ** -0.5
PH = 8
TOPK = 16
NKEYS = 128
PICKS = PH * TOPK
GROUP = 4
GROUPS = PICKS // GROUP
U_SLOTS = 8
V_SLOTS = 16
W_SLOTS = 4
PIECES = 48
PIECE_Q, PIECE_K, PIECE_V, PIECE_XC, PIECE_C, PIECE_B, PIECE_OUT, PIECE_PEER = 0, 4, 8, 12, 16, 20, 24, 32
EPS = 1e-6
MASKED = -1e30
TAKEN = -3e38
MAGIC = float(0x5F3759DF)
FRONT_AT = 2
SLICES = 30
C_G1, C_CONV, C_GCV, C_GSB, C_GQ, C_GK, C_END = 0, 8, 20, 24, 28, 29, 30


def build(nc, x, wstream, chan, keys, norm2_g, peer_u, peer_v, out):
    with ExitStack() as ctx:
        def sb(name, shape, dt=F32):
            return ctx.enter_context(nc.sbuf_tensor(name, shape, dt))

        def ps(name, shape):
            return ctx.enter_context(nc.psum_tensor(name, shape, F32))

        def sem(name):
            return ctx.enter_context(nc.semaphore(name))

        u_ring = sb("u_ring", [P, U_SLOTS, D])
        v_ring = sb("v_ring", [P, V_SLOTS, D])
        w_ring = sb("w_ring", [P, W_SLOTS, 1024])
        kT = sb("kT", [P, CH, S])
        vals_sb = sb("vals_sb", [P, BLOCKS, DSB])
        x_next = sb("x_next", [P, D])
        x_mix = sb("x_mix", [P, D])
        h_next = sb("h_next", [P, D])
        h_mix = sb("h_mix", [P, D])
        hT = sb("hT", [P, KD, P])
        g2_all = sb("g2_all", [P, D])
        ra = sb("ra", [P, S + 1])
        rb = sb("rb", [P, S])
        rc = sb("rc", [P, S])
        rd = sb("rd", [P, S])
        band = sb("band", [P, S + 7 * P], BF16)
        qT = sb("qT", [P, CH, P])
        uT = sb("uT", [P, CH, P + 2])
        cvT = sb("cvT", [P, CH, P])
        sbT = sb("sbT", [P, CH, P])
        diag = sb("diag", [P, 2, GROUP, P])
        keysT = sb("keysT", [P, 2 * NKEYS])
        ident = sb("ident", [P, P])
        ones = sb("ones", [P, 1])
        chan_sb = sb("chan_sb", [P, C_END])
        iota_i = sb("iota_i", [P, TOPK], I32)
        iota_f = sb("iota_f", [P, TOPK])
        top_v = sb("top_v", [P, 2 * PH, TOPK])
        top_i = sb("top_i", [P, 2 * PH, TOPK], U32)
        sum_v = sb("sum_v", [P, PH, TOPK])
        sum_p = sb("sum_p", [P, PH, TOPK], U32)
        top_f = rd[:, 0:256].rearrange("p (c k) -> p c k", c=2 * PH)
        pos = rd[:, 256:512].bitcast(U32).rearrange("p (i k) -> p i k", i=2)
        pos_f = rd[:, 512:768].rearrange("p (i k) -> p i k", i=2)
        sel = rd[:, 768:1024].rearrange("p (i k) -> p i k", i=2)
        gate_e = sb("gate_e", [P, PH, TOPK])
        gate_next = sb("gate_next", [P, PH, TOPK])
        gate_mix = sb("gate_mix", [P, PICKS])
        den = sb("den", [P, PH])
        rden = sb("rden", [P, PH])
        idx_next = sb("idx_next", [P, PICKS], U32)
        idx_mix = sb("idx_mix", [P, PICKS], U32)
        idx_now = sb("idx_now", [P, 2, V_SLOTS], U32)
        ss = sb("ss", [P, 2 * HEADS])
        rs_a = sb("rs_a", [P, 2 * HEADS])
        rs_t = sb("rs_t", [P, 2 * HEADS])
        inv1 = sb("inv1", [P, 1])
        invqk = sb("invqk", [P, 2 * HEADS])
        ss2 = sb("ss2", [P, 2])
        inv2 = sb("inv2", [P, 2])
        invh = sb("invh", [P, 1])
        dots = sb("dots", [P, 2, GROUP])
        acts = sb("acts", [P, 2, GROUP])
        wgt = sb("wgt", [P, 2, GROUP])

        acc = ps("acc", [P, D])
        pz = ps("pz", [P, S])
        pt = ps("pt", [P, 1024])
        pm = ps("pm", [P, 1024])
        po = pm[:, 512:1024]

        consts_in = sem("consts_in")
        consts_set = sem("consts_set")
        iota_set = sem("iota_set")
        x_in = sem("x_in")
        w_in = [sem(f"w_in{i}") for i in range(W_SLOTS)]
        piece_done = sem("piece_done")
        norm1 = sem("norm1")
        h_ready = sem("h_ready")
        h_turned = sem("h_turned")
        hT_ready = sem("hT_ready")
        qk_sq = sem("qk_sq")
        qk_norm = sem("qk_norm")
        v_kept = sem("v_kept")
        qk_turned = sem("qk_turned")
        qkT_ready = sem("qkT_ready")
        xc_kept = sem("xc_kept")
        cv_raw = sem("cv_raw")
        cv_sq = sem("cv_sq")
        cvT_ready = sem("cvT_ready")
        cv_ss = sem("cv_ss")
        cv_ss_kept = sem("cv_ss_kept")
        z_psum = sem("z_psum")
        z_masked = sem("z_masked")
        beta_ready = sem("beta_ready")
        a_ready = sem("a_ready")
        a_turned = sem("a_turned")
        aT_ready = sem("aT_ready")
        av_done = sem("av_done")
        sb_kept = sem("sb_kept")
        sb_turned = sem("sb_turned")
        sbT_ready = sem("sbT_ready")
        h2_ready = sem("h2_ready")
        h2_turned = sem("h2_turned")
        h2T_ready = sem("h2T_ready")
        pq_ready = sem("pq_ready")
        s_psum = sem("s_psum")
        s_ready = sem("s_ready")
        s_ranked = sem("s_ranked")
        gate_arg = sem("gate_arg")
        gate_exp = sem("gate_exp")
        picks_ready = sem("picks_ready")
        idx_taken = sem("idx_taken")
        idx_slice = sem("idx_slice")
        h_mix_set = sem("h_mix_set")
        x_mix_set = sem("x_mix_set")
        u_in = [sem(f"u_in{i}") for i in range(U_SLOTS)]
        v_in = [sem(f"v_in{i}") for i in range(V_SLOTS)]
        dots_done = sem("dots_done")
        gelu_done = sem("gelu_done")
        wgt_ready = sem("wgt_ready")
        diag_ready = sem("diag_ready")
        group_done = sem("group_done")
        acc_free = sem("acc_free")
        x_mix_free = sem("x_mix_free")
        y_out = sem("y_out")
        passed = sem("passed")
        own_v = sem("own_v")

        def wait(eng, s, value):
            if not (isinstance(value, int) and value <= 0):
                eng.wait_ge(s, value)

        def apart(eng):
            eng.sem_inc(passed, 1)

        def grid(ap, n):
            return ap.rearrange("p (a b) -> p a b", a=n)

        def spread(ap, n):
            return ap.unsqueeze(2).to_broadcast([ap.shape[0], ap.shape[1], n])

        block = ctx.enter_context(nc.Block())

        @block.sync
        def _(sp):
            sp.dma_start(chan_sb[:], chan).then_inc(consts_in, 16)
            sp.dma_start(keysT[:], keys).then_inc(consts_in, 16)
            sp.dma_start(g2_all[:], norm2_g.to_broadcast([P, D])).then_inc(consts_in, 16)

            def loads(b):
                wait(sp, x_mix_set, b)
                sp.dma_start(x_next[:], x[bass.ds(b * P, P), :]).then_inc(x_in, 16)
                for j in range(PIECES):
                    wait(sp, piece_done, b * PIECES + j - W_SLOTS + 1)
                    sp.dma_start(w_ring[:, j % W_SLOTS, :], wstream[j]).then_inc(w_in[j % W_SLOTS], 16)

            def store(b):
                sp.wait_ge(acc_free, b + 2)
                sp.dma_start(out[bass.ds(b * P, P), :], x_mix[:]).then_inc(y_out, 16)
                sp.wait_ge(y_out, 16 * (b + 1))
                sp.sem_inc(x_mix_free, 1)

            sp.sem_inc(x_mix_free, 1)
            loads(0)
            with sp.Fori(1, BLOCKS) as b:
                loads(b)
                store(b - 1)
            store(BLOCKS - 1)
            sp.wait_ge(y_out, 16 * BLOCKS)

        @block.gpsimd
        def _(pool):
            nc.gpsimd.memset(ident[:], 0.0).then_inc(consts_set, 1)
            nc.gpsimd.memset(band[:], 0.0).then_inc(consts_set, 1)
            nc.gpsimd.iota(iota_i[:], [[1, TOPK]], base=0, channel_multiplier=0).then_inc(iota_set, 1)
            nc.gpsimd.memset(ones[:], 1.0).then_inc(consts_set, 1)
            pool.wait_ge(consts_set, 3)
            nc.gpsimd.affine_select(out=ident[:], in_=ident[:], compare_op=ALU.not_equal, fill=1.0, base=0,
                                    pattern=[[-1, P]], channel_multiplier=1).then_inc(consts_set, 1)
            nc.gpsimd.affine_select(out=band[:], in_=band[:], compare_op=ALU.is_gt, fill=MASKED,
                                    base=(BLOCKS - 1) * P, pattern=[[-1, S + 7 * P]],
                                    channel_multiplier=1).then_inc(consts_set, 1)

            def take(b):
                pool.wait_ge(picks_ready, b + 1)
                apart(pool)
                nc.gpsimd.tensor_copy(idx_mix[:], idx_next[:]).then_inc(idx_taken, 1)
                pool.wait_ge(idx_taken, b + 1)
                apart(pool)

            def two_rounds(b, m):
                for r in range(2):
                    first = m * 2 * V_SLOTS + r * V_SLOTS
                    nc.gpsimd.tensor_copy(idx_now[:, r, :], idx_mix[:, bass.ds(first, V_SLOTS)]).then_inc(idx_slice, 1)
                    pool.wait_ge(idx_slice, (b * (PICKS // V_SLOTS)) + 2 * m + r + 1)
                    apart(pool)
                    for g in range(V_SLOTS // GROUP):
                        n = b * GROUPS + (2 * m + r) * (V_SLOTS // GROUP) + g
                        wait(pool, dots_done, n + 1 - U_SLOTS // GROUP)
                        apart(pool)
                        for j in range(g * GROUP, (g + 1) * GROUP):
                            nc.gpsimd.indirect_dma_start(
                                out=u_ring[:, j % U_SLOTS, :], out_offset=None, in_=peer_u,
                                in_offset=bass.IndirectOffsetOnAxis(ap=idx_now[:, r, j:j + 1], axis=0),
                            ).then_inc(u_in[j % U_SLOTS], 16)
                        wait(pool, group_done, n + 1 - V_SLOTS // GROUP)
                        apart(pool)
                        for j in range(g * GROUP, (g + 1) * GROUP):
                            nc.gpsimd.indirect_dma_start(
                                out=v_ring[:, j, :], out_offset=None, in_=peer_v,
                                in_offset=bass.IndirectOffsetOnAxis(ap=idx_now[:, r, j:j + 1], axis=0),
                            ).then_inc(v_in[j], 16)

            rounds = PICKS // (2 * V_SLOTS)
            take(0)
            two_rounds(0, 0)
            with pool.Fori(1, rounds) as m:
                two_rounds(0, m)
            with pool.Fori(1, BLOCKS) as b:
                take(b)
                with pool.Fori(0, rounds) as m:
                    two_rounds(b, m)

        @block.tensor
        def _(pe):
            def piece(b, j):
                pe.wait_ge(w_in[j % W_SLOTS], 16 * (b * (PIECES // W_SLOTS) + j // W_SLOTS + 1))
                return w_ring[:, j % W_SLOTS, :]

            def rows(b, first, o, o2=None):
                for j in range(4):
                    w = piece(b, first + j)
                    for i in range(2):
                        k = 2 * j + i
                        mm = nc.tensor.matmul(o, hT[:, k, :], w[:, i * 512:(i + 1) * 512],
                                              start=(k == 0), stop=(k == KD - 1))
                    mm.then_inc(piece_done, 1)

            def columns(b, first, o):
                for c in range(4):
                    w = piece(b, first + c)
                    for k in range(KD):
                        mm = nc.tensor.matmul(o[:, c * P:(c + 1) * P], w[:, k * P:(k + 1) * P], hT[:, k, :],
                                              start=(k == 0), stop=(k == KD - 1))
                    mm.then_inc(piece_done, 1)

            def turn(dst, src, tiles):
                for t in range(tiles):
                    mm = nc.tensor.transpose(dst[:, t * P:(t + 1) * P], src[:, t * P:(t + 1) * P], ident[:])
                return mm

            def attend(b, i):
                if i >= 2:
                    h = i - 2
                    pe.wait_ge(aT_ready, b * HEADS + h + 1)
                    for t in range(BLOCKS):
                        mm = nc.tensor.matmul(po[:, h * DH:(h + 1) * DH], rd[:, t * P:(t + 1) * P],
                                              vals_sb[:, t, h * DH:(h + 1) * DH],
                                              start=(t == 0), stop=(t == BLOCKS - 1))
                    mm.then_inc(av_done, 1)
                if i < HEADS:
                    if i == 0:
                        pe.wait_ge(v_kept, b + 1)
                        pe.wait_ge(cv_raw, b + 1)
                        pe.wait_ge(qkT_ready, 2 * b + 2)
                    wait(pe, z_masked, b * HEADS + i)
                    r = DH * (i % 2)
                    for half in range(2):
                        mm = nc.tensor.matmul(pz[:, half * 512:(half + 1) * 512], qT[r:r + DH, i // 2, :],
                                              kT[r:r + DH, i // 2, half * 512:(half + 1) * 512],
                                              start=True, stop=True)
                    mm.then_inc(z_psum, 1)
                if 1 <= i <= HEADS:
                    pe.wait_ge(a_ready, b * HEADS + i)
                    wait(pe, aT_ready, b * HEADS + i - 1)
                    turn(pt, rb, BLOCKS).then_inc(a_turned, 1)

            def front(b, s):
                if s == 0:
                    pe.wait_ge(h_ready, b + 1)
                    wait(pe, h2T_ready, b)
                    turn(pt, ra, KD).then_inc(h_turned, 1)
                if s == 1:
                    pe.wait_ge(hT_ready, b + 1)
                    wait(pe, s_ready, b * 4)
                    rows(b, PIECE_Q, pm[:, 0:512])
                    rows(b, PIECE_K, pm[:, 512:1024])
                if s == 2:
                    rows(b, PIECE_V, pz[:, 0:512])
                if s == 3:
                    pe.wait_ge(qk_norm, 2 * b + 2)
                    turn(pt, rb, 8).then_inc(qk_turned, 1)
                    columns(b, PIECE_XC, pm[:, 0:512])
                    columns(b, PIECE_C, pm[:, 512:1024])
                if s == 4:
                    columns(b, PIECE_B, pz[:, 512:1024])
                if s == 5:
                    pe.wait_ge(cv_sq, b + 1)
                    for c in range(CH):
                        mm = nc.tensor.matmul(pm[:, 0:1], rc[:, 512 + c * P:512 + (c + 1) * P], ones[:],
                                              start=(c == 0), stop=(c == CH - 1))
                    mm.then_inc(cv_ss, 1)
                if 5 <= s < 5 + HEADS + 2:
                    attend(b, s - 5)
                if s == 16:
                    pe.wait_ge(sb_kept, b + 1)
                    turn(pt, rd, CH).then_inc(sb_turned, 1)
                if s == 17:
                    pe.wait_ge(sbT_ready, b + 1)
                    pe.wait_ge(cvT_ready, b + 1)
                    pe.wait_ge(cv_ss_kept, b + 1)
                    for n, o in enumerate((pm, pz)):
                        for j in range(4):
                            w = piece(b, PIECE_OUT + 4 * n + j)
                            src, bank = (sbT, o[:, 0:512]) if j < 2 else (cvT, o[:, 512:1024])
                            for i in range(2):
                                c = (2 * j + i) % CH
                                mm = nc.tensor.matmul(bank, src[:, c, :], w[:, i * 512:(i + 1) * 512],
                                                      start=(c == 0), stop=(c == CH - 1))
                            mm.then_inc(piece_done, 1)
                if s == 19:
                    pe.wait_ge(h2_ready, b + 1)
                    turn(pt, h_next, KD).then_inc(h2_turned, 1)
                if 20 <= s < 24:
                    q = s - 20
                    if q == 0:
                        pe.wait_ge(h2T_ready, b + 1)
                    if q >= 2:
                        pe.wait_ge(pq_ready, 4 * b + q - 1)
                    columns(b, PIECE_PEER + 4 * q, pm[:, (q % 2) * 512:(q % 2) * 512 + 512])
                if 21 <= s < 25:
                    q = s - 21
                    pe.wait_ge(pq_ready, 4 * b + q + 1)
                    if q >= 2:
                        pe.wait_ge(s_ready, 4 * b + q - 1)
                    o = (q % 2) * 512
                    for c in range(4):
                        mm = nc.tensor.matmul(pz[:, o + c * P:o + (c + 1) * P], rd[:, o + c * P:o + (c + 1) * P],
                                              keysT[:, (c % 2) * NKEYS:(c % 2 + 1) * NKEYS],
                                              start=True, stop=True)
                    mm.then_inc(s_psum, 1)

            def mix(b, n):
                pe.wait_ge(diag_ready, b * GROUPS + n + 1)
                if n == 0:
                    pe.wait_ge(acc_free, b + 1)
                for j in range(GROUP):
                    k = n * GROUP + j
                    pe.wait_ge(v_in[k % V_SLOTS], 16 * (b * (PICKS // V_SLOTS) + k // V_SLOTS + 1))
                    for half in range(2):
                        mm = nc.tensor.matmul(acc[:, half * 512:(half + 1) * 512], diag[:, n % 2, j, :],
                                              v_ring[:, k % V_SLOTS, half * 512:(half + 1) * 512],
                                              start=(k == 0), stop=(k == PICKS - 1))
                mm.then_inc(group_done, 1)

            pe.wait_ge(consts_in, 48)
            pe.wait_ge(consts_set, 5)
            for s in range(SLICES):
                front(0, s)
            with pe.Fori(1, BLOCKS) as b:
                for n in range(GROUPS):
                    if n >= 1:
                        mix(b - 1, n - 1)
                    if n >= FRONT_AT:
                        front(b, n - FRONT_AT)
                mix(b - 1, GROUPS - 1)
            for n in range(GROUPS):
                mix(BLOCKS - 1, n)

        @block.scalar
        def _(act):
            copy = ACT.Copy

            def front(b, s):
                if s == 0:
                    act.wait_ge(norm1, b + 1)
                    nc.scalar.activation(ra[:, 0:D], x_next[:], copy, scale=inv1[:]).then_inc(h_ready, 1)
                if s == 1:
                    for i in range(2):
                        act.wait_ge(piece_done, b * PIECES + PIECE_Q + 4 * (i + 1))
                        nc.scalar.activation(rc[:, i * 512:(i + 1) * 512], pm[:, i * 512:(i + 1) * 512],
                                             ACT.Square).then_inc(qk_sq, 1)
                if s == 2:
                    act.wait_ge(piece_done, b * PIECES + PIECE_V + 4)
                    nc.scalar.activation(vals_sb[:, bass.ds(b, 1), :], pz[:, 0:512].unsqueeze(1),
                                         copy).then_inc(v_kept, 1)
                if s == 3:
                    act.wait_ge(qk_turned, b + 1)
                    nc.scalar.activation(qT[:], grid(pt[:, 0:512], CH), copy,
                                         scale=chan_sb[:, C_GQ:C_GQ + 1]).then_inc(qkT_ready, 1)
                    nc.scalar.activation(kT[:, :, bass.ds(b * P, P)], grid(pt[:, 512:1024], CH), copy,
                                         scale=chan_sb[:, C_GK:C_GK + 1]).then_inc(qkT_ready, 1)
                    act.wait_ge(piece_done, b * PIECES + PIECE_XC + 4)
                    nc.scalar.activation(rc[:, 0:512], pm[:, 0:512], copy).then_inc(xc_kept, 1)
                if s == 4:
                    act.wait_ge(cv_raw, b + 1)
                    nc.scalar.activation(rc[:, 512:1024], rc[:, 0:512], ACT.Square).then_inc(cv_sq, 1)
                if 5 <= s < 5 + HEADS + 1:
                    i = s - 5
                    if i >= 1:
                        act.wait_ge(a_turned, b * HEADS + i)
                        wait(act, av_done, b * HEADS + i - 1)
                        if i == 1:
                            wait(act, s_psum, 4 * b)
                        nc.scalar.activation(rd[:], pt[:], copy).then_inc(aT_ready, 1)
                    if i < HEADS:
                        act.wait_ge(z_masked, b * HEADS + i + 1)
                        if i == 0:
                            act.wait_ge(cv_ss, b + 1)
                            act.wait_ge(cvT_ready, b + 1)
                        nc.scalar.activation(rb[:], ra[:, 0:S], ACT.Sigmoid, scale=SCALE)
                        nc.scalar.activation(rc[:], ra[:, 0:S], ACT.Sigmoid, scale=-SCALE).then_inc(beta_ready, 1)
                if s == 15:
                    act.wait_ge(av_done, (b + 1) * HEADS)
                    nc.scalar.activation(rd[:, 0:512], po, copy).then_inc(sb_kept, 1)
                if s == 19:
                    act.wait_ge(h2_turned, b + 1)
                    nc.scalar.activation(hT[:], grid(pt[:], KD), copy).then_inc(h2T_ready, 1)
                if 21 <= s < 25:
                    q, o = s - 21, ((s - 21) % 2) * 512
                    act.wait_ge(s_psum, 4 * b + q + 1)
                    if q >= 2:
                        act.wait_ge(s_ranked, 4 * b + q - 1)
                    nc.scalar.activation(rb[:, o:o + 512], pz[:, o:o + 512], copy).then_inc(s_ready, 1)
                if 20 <= s < 24:
                    q, o = s - 20, ((s - 20) % 2) * 512
                    act.wait_ge(piece_done, b * PIECES + PIECE_PEER + 4 * (q + 1))
                    if q == 0:
                        act.wait_ge(sb_turned, b + 1)
                    nc.scalar.activation(rd[:, o:o + 512], pm[:, o:o + 512], copy).then_inc(pq_ready, 1)
                if s == 28:
                    act.wait_ge(gate_arg, b + 1)
                    nc.scalar.activation(gate_e[:], gate_e[:], ACT.Exp).then_inc(gate_exp, 1)

            def diagonals(b, n):
                act.wait_ge(wgt_ready, b * GROUPS + n + 1)
                if n == 0:
                    act.wait_ge(acc_free, b + 1)
                else:
                    wait(act, group_done, b * GROUPS + n - 1)
                for j in range(GROUP):
                    a = nc.scalar.activation(diag[:, n % 2, j, :], ident[:], copy, scale=wgt[:, n % 2, j:j + 1])
                a.then_inc(diag_ready, 1)

            def gelu(b, n):
                act.wait_ge(dots_done, b * GROUPS + n + 1)
                nc.scalar.activation(acts[:, n % 2, :], dots[:, n % 2, :], ACT.Gelu).then_inc(gelu_done, 1)

            def take(b):
                act.wait_ge(picks_ready, b + 1)
                nc.scalar.activation(h_mix[:], h_next[:], copy).then_inc(h_mix_set, 1)
                nc.scalar.activation(gate_mix[:], gate_next[:].rearrange("p h k -> p (h k)"),
                                     copy).then_inc(h_mix_set, 1)

            def take_residual(b):
                act.wait_ge(x_mix_free, b + 1)
                nc.scalar.activation(x_mix[:], x_next[:], copy).then_inc(x_mix_set, 1)

            act.wait_ge(consts_in, 48)
            act.wait_ge(consts_set, 5)
            for s in range(SLICES):
                front(0, s)
            with act.Fori(1, BLOCKS) as b:
                take(b - 1)
                for n in range(GROUPS):
                    if n >= 1:
                        diagonals(b - 1, n - 1)
                    gelu(b - 1, n)
                    if n == FRONT_AT - 1:
                        take_residual(b - 1)
                    if n >= FRONT_AT:
                        front(b, n - FRONT_AT)
                diagonals(b - 1, GROUPS - 1)
            take(BLOCKS - 1)
            for n in range(GROUPS):
                if n >= 1:
                    diagonals(BLOCKS - 1, n - 1)
                gelu(BLOCKS - 1, n)
                if n == FRONT_AT - 1:
                    take_residual(BLOCKS - 1)
            diagonals(BLOCKS - 1, GROUPS - 1)

        @block.vector
        def _(dve):
            V = nc.vector
            count = {"here": 0, "front": 0}

            def step(ins):
                ins.then_inc(own_v, 1)
                count["here"] += 1

            def settle(b):
                dve.wait_ge(own_v, b * count["front"] + count["here"])

            def inverse_root(b, o, sums, n, scale, done=None):
                a, t = rs_a[:, 0:n], rs_t[:, 0:n]
                step(V.tensor_scalar(a, sums, scale, EPS, ALU.mult, ALU.add))
                settle(b)
                step(V.tensor_scalar(o.bitcast(I32), a.bitcast(I32), 1, None, ALU.logical_shift_right))
                settle(b)
                step(V.tensor_scalar(o.bitcast(I32), o.bitcast(I32), -1.0, MAGIC, ALU.mult, ALU.add))
                settle(b)
                for i in range(4):
                    step(V.tensor_tensor(t, o, o, ALU.mult))
                    settle(b)
                    step(V.scalar_tensor_tensor(t, t, -0.5, a, ALU.mult, ALU.mult))
                    settle(b)
                    last = V.scalar_tensor_tensor(o, t, 1.5, o, ALU.add, ALU.mult)
                    if i == 3 and done is not None:
                        last.then_inc(done, 1)
                    else:
                        step(last)
                        settle(b)

            def square_sum(b, src, junk, o):
                step(V.tensor_tensor_reduce(junk, src, src, 1.0, 0.0, ALU.mult, ALU.add, o))

            def attend(b, i):
                if 1 <= i <= HEADS:
                    dve.wait_ge(beta_ready, b * HEADS + i)
                    step(V.tensor_tensor_scan(ra[:, 0:S][:, ::-1], rc[:, ::-1], rc[:, ::-1], 1.0,
                                              ALU.mult, ALU.bypass))
                    settle(b)
                    V.tensor_tensor(rb[:], rb[:], ra[:, 1:S + 1], ALU.mult).then_inc(a_ready, 1)
                if i < HEADS:
                    dve.wait_ge(z_psum, b * HEADS + i + 1)
                    if 1 <= i:
                        dve.wait_ge(a_ready, b * HEADS + i)
                    apart(dve)
                    V.tensor_tensor(ra[:, 0:S], pz[:], band[:, bass.ds((BLOCKS - 1 - b) * P, S)],
                                    ALU.add).then_inc(z_masked, 1)

            def rank(b, q):
                dve.wait_ge(s_ready, 4 * b + q + 1)
                o = (q % 2) * 512
                apart(dve)
                row = lambda r, c: r[:, o + c * NKEYS:o + (c + 1) * NKEYS]
                for c in range(4):
                    step(V.max(top_v[:, 4 * q + c, 0:8], row(rb, c)))
                settle(b)
                apart(dve)
                for c in range(4):
                    step(V.max_index(top_i[:, 4 * q + c, 0:8], top_v[:, 4 * q + c, 0:8], row(rb, c)))
                for c in range(4):
                    step(V.match_replace(row(rc, c), top_v[:, 4 * q + c, 0:8], row(rb, c), TAKEN))
                settle(b)
                apart(dve)
                for c in range(4):
                    step(V.max(top_v[:, 4 * q + c, 8:16], row(rc, c)))
                settle(b)
                apart(dve)
                for c in range(4):
                    i = V.max_index(top_i[:, 4 * q + c, 8:16], top_v[:, 4 * q + c, 8:16], row(rc, c))
                i.then_inc(s_ranked, 1)

            def combine(b, q):
                if q == 0:
                    dve.wait_ge(s_ranked, 4 * (b + 1))
                h0 = 4 * q
                first = top_v[:, 2 * h0:2 * h0 + 8:2, :].unsqueeze(3).to_broadcast([P, 4, TOPK, TOPK])
                second = top_v[:, 2 * h0 + 1:2 * h0 + 8:2, :].unsqueeze(2).to_broadcast([P, 4, TOPK, TOPK])
                step(V.tensor_tensor(rc[:].rearrange("p (h i j) -> p h i j", h=4, i=TOPK), first, second, ALU.add))
                settle(b)
                apart(dve)
                row = lambda r, c: r[:, c * 256:(c + 1) * 256]
                for c in range(4):
                    step(V.max(sum_v[:, h0 + c, 0:8], row(rc, c)))
                settle(b)
                apart(dve)
                for c in range(4):
                    step(V.max_index(sum_p[:, h0 + c, 0:8], sum_v[:, h0 + c, 0:8], row(rc, c)))
                for c in range(4):
                    step(V.match_replace(row(ra, c), sum_v[:, h0 + c, 0:8], row(rc, c), TAKEN))
                settle(b)
                apart(dve)
                for c in range(4):
                    step(V.max(sum_v[:, h0 + c, 8:16], row(ra, c)))
                settle(b)
                apart(dve)
                for c in range(4):
                    step(V.max_index(sum_p[:, h0 + c, 8:16], sum_v[:, h0 + c, 8:16], row(ra, c)))
                settle(b)

            def look_up(b):
                flat = sum_p[:].rearrange("p h k -> p (h k)")
                step(V.tensor_scalar(pos[:, 0, :], flat, 4, None, ALU.logical_shift_right))
                step(V.tensor_scalar(pos[:, 1, :], flat, 15, None, ALU.bitwise_and))
                step(V.tensor_copy(top_f[:], top_i[:]))
                settle(b)
                step(V.tensor_copy(pos_f[:], pos[:]))
                settle(b)
                for q in range(2):
                    k0 = q * 64
                    for half, r in ((0, ra), (1, rc)):
                        hot = r[:, 0:1024].rearrange("p (k a) -> p k a", a=TOPK)
                        step(V.tensor_tensor(hot, iota_f[:].unsqueeze(1).to_broadcast([P, 64, TOPK]),
                                             spread(pos_f[:, half, k0:k0 + 64], TOPK), ALU.is_equal))
                    settle(b)
                    for half, r in ((0, ra), (1, rc)):
                        hot = r[:, 0:1024].rearrange("p (h k a) -> p h k a", h=4, a=TOPK)
                        step(V.tensor_tensor(hot, hot, top_f[:, 8 * q + half:8 * q + 8:2, :].unsqueeze(2)
                                             .to_broadcast([P, 4, TOPK, TOPK]), ALU.mult))
                    settle(b)
                    for half, r in ((0, ra), (1, rc)):
                        hot = r[:, 0:1024].rearrange("p (k a) -> p k a", a=TOPK)
                        step(V.tensor_reduce(sel[:, half, k0:k0 + 64], hot, AX_X, ALU.add))
                    settle(b)

            def front(b, s):
                if s == 0:
                    dve.wait_ge(x_in, 16 * (b + 1))
                    square_sum(b, x_next[:], ra[:, 0:D], ss[:, 0:1])
                    settle(b)
                    inverse_root(b, inv1[:], ss[:, 0:1], 1, 1.0 / D, done=norm1)
                if s == 1:
                    dve.wait_ge(h_turned, b + 1)
                    V.tensor_tensor(hT[:], grid(pt[:], KD), spread(chan_sb[:, C_G1:C_G1 + KD], P),
                                    ALU.mult).then_inc(hT_ready, 1)
                if s == 2:
                    dve.wait_ge(qk_sq, 2 * (b + 1))
                    step(V.tensor_reduce(ss[:], grid(rc[:], 2 * HEADS), AX_X, ALU.add))
                    settle(b)
                    inverse_root(b, invqk[:], ss[:], 2 * HEADS, 1.0 / DH)
                    for i in range(2):
                        V.tensor_tensor(grid(rb[:, i * 512:(i + 1) * 512], HEADS),
                                        grid(pm[:, i * 512:(i + 1) * 512], HEADS),
                                        spread(invqk[:, i * HEADS:(i + 1) * HEADS], DH),
                                        ALU.mult).then_inc(qk_norm, 1)
                if s == 3:
                    step(V.tensor_copy(uT[:, :, 0:2], uT[:, :, P:P + 2]))
                    settle(b)
                    dve.wait_ge(xc_kept, b + 1)
                    dve.wait_ge(piece_done, b * PIECES + PIECE_C + 4)
                    step(V.tensor_tensor(uT[:, :, 2:P + 2], grid(pm[:, 512:1024], CH), grid(rc[:, 0:512], CH),
                                         ALU.mult))
                if s == 4:
                    y = grid(rc[:, 512:1024], CH)
                    tap = lambda w, c: chan_sb[:, C_CONV + w * CH + c:C_CONV + w * CH + c + 1]
                    settle(b)
                    for c in range(CH):
                        step(V.tensor_scalar(y[:, c, :], uT[:, c, 0:P], tap(0, c), None, ALU.mult))
                    for w in (1, 2):
                        settle(b)
                        for c in range(CH):
                            step(V.scalar_tensor_tensor(y[:, c, :], uT[:, c, w:w + P], tap(w, c), y[:, c, :],
                                                        ALU.mult, ALU.add))
                    settle(b)
                    dve.wait_ge(piece_done, b * PIECES + PIECE_B + 4)
                    V.tensor_tensor(grid(rc[:, 0:512], CH), grid(pz[:, 512:1024], CH), y,
                                    ALU.mult).then_inc(cv_raw, 1)
                    dve.wait_ge(cv_raw, b + 1)
                    V.tensor_tensor(cvT[:], grid(rc[:, 0:512], CH), spread(chan_sb[:, C_GCV:C_GCV + CH], P),
                                    ALU.mult).then_inc(cvT_ready, 1)
                if s == 5:
                    dve.wait_ge(cv_ss, b + 1)
                    V.tensor_copy(ss2[:, 1:2], pm[:, 0:1]).then_inc(cv_ss_kept, 1)
                if 5 <= s < 5 + HEADS + 1:
                    attend(b, s - 5)
                if s == 15:
                    dve.wait_ge(sb_kept, b + 1)
                    square_sum(b, rd[:, 0:512], rb[:, 0:512], ss2[:, 0:1])
                    settle(b)
                    inverse_root(b, inv2[:], ss2[:], 2, 1.0 / DSB)
                if s == 16:
                    dve.wait_ge(sb_turned, b + 1)
                    V.tensor_tensor(sbT[:], grid(pt[:, 0:512], CH), spread(chan_sb[:, C_GSB:C_GSB + CH], P),
                                    ALU.mult).then_inc(sbT_ready, 1)
                if s == 18:
                    for n, o in enumerate((pm, pz)):
                        dve.wait_ge(piece_done, b * PIECES + PIECE_OUT + 4 * (n + 1))
                        xs = x_next[:, n * 512:(n + 1) * 512]
                        step(V.scalar_tensor_tensor(xs, o[:, 0:512], inv2[:, 0:1], xs, ALU.mult, ALU.add))
                        settle(b)
                        step(V.scalar_tensor_tensor(xs, o[:, 512:1024], inv2[:, 1:2], xs, ALU.mult, ALU.add))
                    settle(b)
                    square_sum(b, x_next[:], ra[:, 0:D], ss[:, 0:1])
                    settle(b)
                    inverse_root(b, invh[:], ss[:, 0:1], 1, 1.0 / D)
                    V.scalar_tensor_tensor(h_next[:], x_next[:], invh[:], g2_all[:], ALU.mult,
                                           ALU.mult).then_inc(h2_ready, 1)
                if 22 <= s < 26:
                    rank(b, s - 22)
                if s in (26, 27):
                    combine(b, s - 26)
                if s == 27:
                    V.tensor_tensor(gate_e[:], sum_v[:], sum_v[:, :, 0:1].to_broadcast([P, PH, TOPK]),
                                    ALU.subtract).then_inc(gate_arg, 1)
                if s == 28:
                    look_up(b)
                if s == 29:
                    dve.wait_ge(gate_exp, b + 1)
                    step(V.tensor_reduce(den[:], gate_e[:], AX_X, ALU.add))
                    settle(b)
                    step(V.reciprocal(rden[:], den[:]))
                    settle(b)
                    wait(dve, h_mix_set, 2 * b)
                    step(V.tensor_tensor(gate_next[:], gate_e[:], spread(rden[:], TOPK), ALU.mult))
                    wait(dve, idx_taken, b)
                    V.scalar_tensor_tensor(idx_next[:], sel[:, 0, :], float(NKEYS), sel[:, 1, :], ALU.mult,
                                           ALU.add).then_inc(picks_ready, 1)

            def weights(b, n):
                dve.wait_ge(gelu_done, b * GROUPS + n + 1)
                V.tensor_tensor(wgt[:, n % 2, :], acts[:, n % 2, :], gate_mix[:, n * GROUP:(n + 1) * GROUP],
                                ALU.mult).then_inc(wgt_ready, 1)

            def dot(b, n):
                for j in range(GROUP):
                    k = n * GROUP + j
                    dve.wait_ge(u_in[k % U_SLOTS], 16 * (b * (PICKS // U_SLOTS) + k // U_SLOTS + 1))
                    u = u_ring[:, k % U_SLOTS, :]
                    d = V.tensor_tensor_reduce(u, u, h_mix[:], 1.0, 0.0, ALU.mult, ALU.add,
                                               dots[:, n % 2, j:j + 1])
                d.then_inc(dots_done, 1)

            def finish(b):
                dve.wait_ge(group_done, (b + 1) * GROUPS)
                dve.wait_ge(x_mix_set, b + 1)
                V.tensor_tensor(x_mix[:], acc[:], x_mix[:], ALU.add).then_inc(acc_free, 1)

            dve.sem_inc(acc_free, 1)
            step(V.memset(ra[:, S:S + 1], 1.0))
            step(V.memset(uT[:], 0.0))
            step(V.memset(kT[:], 0.0))
            step(V.memset(vals_sb[:], 0.0))
            dve.wait_ge(iota_set, 1)
            step(V.tensor_copy(iota_f[:], iota_i[:]))
            settle(0)
            set_up = count["here"]
            dve.wait_ge(consts_in, 48)
            dve.wait_ge(consts_set, 5)
            for s in range(SLICES):
                front(0, s)
            count["front"] = count["here"] - set_up
            with dve.Fori(1, BLOCKS) as b:
                count["here"] = set_up
                dve.wait_ge(h_mix_set, 2 * b)
                for n in range(GROUPS):
                    if n >= 1:
                        weights(b - 1, n - 1)
                    dot(b - 1, n)
                    if n >= FRONT_AT:
                        front(b, n - FRONT_AT)
                weights(b - 1, GROUPS - 1)
                finish(b - 1)
            dve.wait_ge(h_mix_set, 2 * BLOCKS)
            for n in range(GROUPS):
                if n >= 1:
                    weights(BLOCKS - 1, n - 1)
                dot(BLOCKS - 1, n)
            weights(BLOCKS - 1, GROUPS - 1)
            finish(BLOCKS - 1)


def kernel(x, norm1_g, w_in, q_norm_g, k_norm_g, conv_w, sb_out_g, conv_out_g, w_out, norm2_g, peer_w_q,
           peer_sub_keys, peer_u, peer_v):
    import numpy as np
    import concourse.bacc as bacc
    from concourse.bass_utils import run_bass_kernel_spmd

    def by_rows(w):
        n = w.shape[1] // 512
        w = w.reshape(4, 2, P, n, 512).transpose(3, 0, 2, 1, 4)
        return w.reshape(4 * n, P, 1024)

    def by_columns(w):
        n = w.shape[1] // P
        return w.reshape(KD, P, n, P).transpose(2, 1, 0, 3).reshape(n, P, 1024)

    a = {k: np.asarray(v)[0] for k, v in dict(
        x=x, norm1_g=norm1_g, w_in=w_in, q_norm_g=q_norm_g, k_norm_g=k_norm_g, conv_w=conv_w, sb_out_g=sb_out_g,
        conv_out_g=conv_out_g, w_out=w_out, peer_w_q=peer_w_q, peer_sub_keys=peer_sub_keys, peer_u=peer_u,
        peer_v=peer_v).items()}
    part = [a["w_in"][:, i * DSB:(i + 1) * DSB] for i in range(6)]
    wstream = np.concatenate([by_rows(part[0]), by_rows(part[1]), by_rows(part[2]), by_columns(part[3]),
                              by_columns(part[5]), by_columns(part[4]), by_rows(a["w_out"]),
                              by_columns(a["peer_w_q"])])
    chan = np.concatenate([
        a["norm1_g"].reshape(KD, P).T, a["conv_w"].reshape(3, CH, P).transpose(2, 0, 1).reshape(P, 3 * CH),
        a["conv_out_g"].reshape(CH, P).T, a["sb_out_g"].reshape(CH, P).T,
        np.concatenate([a["q_norm_g"]] * 2)[:, None], np.concatenate([a["k_norm_g"]] * 2)[:, None]], axis=1)
    arrays = {
        "x_in_dram": a["x"], "wstream": wstream, "chan": chan,
        "keys": a["peer_sub_keys"].transpose(2, 0, 1).reshape(P, 2 * NKEYS), "norm2": np.asarray(norm2_g),
        "table_u": a["peer_u"], "table_v": a["peer_v"],
    }
    arrays = {k: np.ascontiguousarray(v) for k, v in arrays.items()}
    nc = bacc.Bacc("TRN2", target_bir_lowering=False, num_devices=1)
    ins = [nc.dram_tensor(k, v.shape, F32, kind="ExternalInput").ap() for k, v in arrays.items()]
    out = nc.dram_tensor("y_out_dram", (S, D), F32, kind="ExternalOutput").ap()
    build(nc, *ins, out)
    r = run_bass_kernel_spmd(nc, [arrays], core_ids=[0])
    return r.results[0]["y_out_dram"].reshape(1, S, D)
```

```python
from contextlib import ExitStack

import concourse.bass as bass
from concourse import mybir

F32 = mybir.dt.float32
BF16 = mybir.dt.bfloat16
U32 = mybir.dt.uint32
I32 = mybir.dt.int32
ALU = mybir.AluOpType
ACT = mybir.ActivationFunctionType
AX_X = mybir.AxisListType.X

P = 128
D = 1024
S = 1024
BLOCKS = S // P
KD = D // P
HEADS = 8
DH = 64
DSB = HEADS * DH
CH = DSB // P
SCALE = DH ** -0.5
PH = 8
TOPK = 16
NKEYS = 128
PICKS = PH * TOPK
GROUP = 4
GROUPS = PICKS // GROUP
U_SLOTS = 8
V_SLOTS = 16
W_SLOTS = 4
PIECES = 48
PIECE_Q, PIECE_K, PIECE_V, PIECE_XC, PIECE_C, PIECE_B, PIECE_OUT, PIECE_PEER = 0, 4, 8, 12, 16, 20, 24, 32
EPS = 1e-6
MASKED = -1e30
TAKEN = -3e38
MAGIC = float(0x5F3759DF)
S_NORM1 = 0
S_PROJ = 2
S_QK = 5
S_HEAD = 7
S_CONV = 6
S_SB = 16
S_OUT = 17
S_NORM2 = 20
S_PEER = 21
S_RANK = 24
S_JOIN = 27
S_LAST = 29
PIECES_AT = {S_PROJ: (0, 3), S_PROJ + 1: (3, 6), S_PROJ + 2: (6, 9), S_PROJ + 3: (9, 12),
             **{S_CONV + i: (12 + 2 * i, 14 + 2 * i) for i in range(6)},
             S_OUT: (24, 27), S_OUT + 1: (27, 30), S_OUT + 2: (30, 32),
             S_PEER: (32, 35), S_PEER + 1: (35, 38), S_PEER + 2: (38, 41), S_PEER + 3: (41, 44), S_PEER + 4: (44, 48)}
C_G1, C_CONV, C_GCV, C_GSB, C_GQ, C_GK, C_END = 0, 8, 20, 24, 28, 29, 30


def build(nc, x, wstream, chan, keys, norm2_g, peer_u, peer_v, out):
    with ExitStack() as ctx:
        def sb(name, shape, dt=F32):
            return ctx.enter_context(nc.sbuf_tensor(name, shape, dt))

        def ps(name, shape):
            return ctx.enter_context(nc.psum_tensor(name, shape, F32))

        def sem(name):
            return ctx.enter_context(nc.semaphore(name))

        u_ring = sb("u_ring", [P, U_SLOTS, D])
        v_ring = sb("v_ring", [P, V_SLOTS, D])
        w_ring = sb("w_ring", [P, W_SLOTS, 1024])
        kT = sb("kT", [P, CH, S])
        vals_sb = sb("vals_sb", [P, BLOCKS, DSB])
        x_next = sb("x_next", [P, D])
        x_mix = sb("x_mix", [P, D])
        h_next = sb("h_next", [P, D])
        h_mix = sb("h_mix", [P, D])
        hT = sb("hT", [P, KD, P])
        g2_all = sb("g2_all", [P, D])
        ra = sb("ra", [P, S + 1])
        rb = sb("rb", [P, S])
        rc = sb("rc", [P, S])
        rd = sb("rd", [P, S])
        band = sb("band", [P, S + 7 * P], BF16)
        qT = sb("qT", [P, CH, P])
        uT = sb("uT", [P, CH, P + 2])
        cvT = sb("cvT", [P, CH, P])
        sbT = sb("sbT", [P, CH, P])
        diag = sb("diag", [P, 2, GROUP, P])
        keysT = sb("keysT", [P, 2 * NKEYS])
        ident = sb("ident", [P, P])
        ones = sb("ones", [P, 1])
        chan_sb = sb("chan_sb", [P, C_END])
        iota_i = sb("iota_i", [P, TOPK], I32)
        iota_f = sb("iota_f", [P, TOPK])
        top_v = sb("top_v", [P, 2 * PH, TOPK])
        top_i = sb("top_i", [P, 2 * PH, TOPK], U32)
        sum_v = sb("sum_v", [P, PH, TOPK])
        sum_p = sb("sum_p", [P, PH, TOPK], U32)
        top_f = rd[:, 0:256].rearrange("p (c k) -> p c k", c=2 * PH)
        pos = rd[:, 256:512].bitcast(U32).rearrange("p (i k) -> p i k", i=2)
        pos_f = rd[:, 512:768].rearrange("p (i k) -> p i k", i=2)
        sel = rd[:, 768:1024].rearrange("p (i k) -> p i k", i=2)
        gate_e = sb("gate_e", [P, PH, TOPK])
        gate_next = sb("gate_next", [P, PH, TOPK])
        gate_mix = sb("gate_mix", [P, PICKS])
        den = sb("den", [P, PH])
        rden = sb("rden", [P, PH])
        idx_next = sb("idx_next", [P, PICKS], U32)
        idx_mix = sb("idx_mix", [P, PICKS], U32)
        idx_now = sb("idx_now", [P, 2, V_SLOTS], U32)
        ss = sb("ss", [P, 2 * HEADS])
        rs_a = sb("rs_a", [P, 2 * HEADS])
        rs_t = sb("rs_t", [P, 2 * HEADS])
        inv1 = sb("inv1", [P, 1])
        invqk = sb("invqk", [P, 2 * HEADS])
        ss2 = sb("ss2", [P, 2])
        inv2 = sb("inv2", [P, 2])
        invh = sb("invh", [P, 1])
        dots = sb("dots", [P, 2, GROUP])
        acts = sb("acts", [P, 2, GROUP])
        wgt = sb("wgt", [P, 2, GROUP])

        acc = ps("acc", [P, D])
        pz = ps("pz", [P, S])
        pt = ps("pt", [P, 1024])
        pm = ps("pm", [P, 1024])
        po = pm[:, 512:1024]

        consts_in = sem("consts_in")
        consts_set = sem("consts_set")
        iota_set = sem("iota_set")
        x_in = sem("x_in")
        residual_in = sem("residual_in")
        w_in = [sem(f"w_in{i}") for i in range(W_SLOTS)]
        piece_done = sem("piece_done")
        norm1 = sem("norm1")
        h_ready = sem("h_ready")
        h_turned = sem("h_turned")
        hT_ready = sem("hT_ready")
        qk_sq = sem("qk_sq")
        qk_norm = sem("qk_norm")
        v_kept = sem("v_kept")
        qk_turned = sem("qk_turned")
        qkT_ready = sem("qkT_ready")
        xc_kept = sem("xc_kept")
        u_ready = sem("u_ready")
        cv_raw = sem("cv_raw")
        cv_sq = sem("cv_sq")
        cvT_ready = sem("cvT_ready")
        cv_ss = sem("cv_ss")
        cv_ss_kept = sem("cv_ss_kept")
        z_psum = sem("z_psum")
        z_masked = sem("z_masked")
        beta_ready = sem("beta_ready")
        a_ready = sem("a_ready")
        a_turned = sem("a_turned")
        aT_ready = sem("aT_ready")
        av_done = sem("av_done")
        sb_kept = sem("sb_kept")
        sb_turned = sem("sb_turned")
        sbT_ready = sem("sbT_ready")
        h2_ready = sem("h2_ready")
        h2_turned = sem("h2_turned")
        h2T_ready = sem("h2T_ready")
        pq_ready = sem("pq_ready")
        s_psum = sem("s_psum")
        s_ready = sem("s_ready")
        s_ranked = sem("s_ranked")
        gate_arg = sem("gate_arg")
        gate_exp = sem("gate_exp")
        picks_ready = sem("picks_ready")
        idx_taken = sem("idx_taken")
        idx_slice = sem("idx_slice")
        h_mix_set = sem("h_mix_set")
        x_mix_set = sem("x_mix_set")
        u_in = [sem(f"u_in{i}") for i in range(U_SLOTS)]
        v_in = [sem(f"v_in{i}") for i in range(V_SLOTS)]
        dots_done = sem("dots_done")
        gelu_done = sem("gelu_done")
        wgt_ready = sem("wgt_ready")
        diag_ready = sem("diag_ready")
        group_done = sem("group_done")
        acc_free = sem("acc_free")
        x_mix_free = sem("x_mix_free")
        y_out = sem("y_out")
        passed = sem("passed")
        own_v = sem("own_v")

        def wait(eng, s, value):
            if not (isinstance(value, int) and value <= 0):
                eng.wait_ge(s, value)

        def apart(eng):
            eng.sem_inc(passed, 1)

        def grid(ap, n):
            return ap.rearrange("p (a b) -> p a b", a=n)

        def spread(ap, n):
            return ap.unsqueeze(2).to_broadcast([ap.shape[0], ap.shape[1], n])

        block = ctx.enter_context(nc.Block())

        @block.sync
        def _(sp):
            sp.dma_start(chan_sb[:], chan).then_inc(consts_in, 16)
            sp.dma_start(keysT[:], keys).then_inc(consts_in, 16)
            sp.dma_start(g2_all[:], norm2_g.to_broadcast([P, D])).then_inc(consts_in, 16)

            def loads(b):
                wait(sp, s_ranked, 4 * b)
                sp.dma_start(rb[:], x[bass.ds(b * P, P), :]).then_inc(x_in, 16)
                for j in range(PIECES):
                    if j == PIECE_OUT - W_SLOTS:
                        wait(sp, x_mix_set, b)
                        sp.dma_start(x_next[:], x[bass.ds(b * P, P), :]).then_inc(residual_in, 16)
                    wait(sp, piece_done, b * PIECES + j - W_SLOTS + 1)
                    sp.dma_start(w_ring[:, j % W_SLOTS, :], wstream[j]).then_inc(w_in[j % W_SLOTS], 16)

            def store(b):
                sp.wait_ge(acc_free, b + 2)
                sp.dma_start(out[bass.ds(b * P, P), :], x_mix[:]).then_inc(y_out, 16)
                sp.wait_ge(y_out, 16 * (b + 1))
                sp.sem_inc(x_mix_free, 1)

            sp.sem_inc(x_mix_free, 1)
            loads(0)
            with sp.Fori(1, BLOCKS) as b:
                loads(b)
                store(b - 1)
            store(BLOCKS - 1)
            sp.wait_ge(y_out, 16 * BLOCKS)

        @block.gpsimd
        def _(pool):
            nc.gpsimd.memset(ident[:], 0.0).then_inc(consts_set, 1)
            nc.gpsimd.memset(band[:], 0.0).then_inc(consts_set, 1)
            nc.gpsimd.iota(iota_i[:], [[1, TOPK]], base=0, channel_multiplier=0).then_inc(iota_set, 1)
            nc.gpsimd.memset(ones[:], 1.0).then_inc(consts_set, 1)
            pool.wait_ge(consts_set, 3)
            nc.gpsimd.affine_select(out=ident[:], in_=ident[:], compare_op=ALU.not_equal, fill=1.0, base=0,
                                    pattern=[[-1, P]], channel_multiplier=1).then_inc(consts_set, 1)
            nc.gpsimd.affine_select(out=band[:], in_=band[:], compare_op=ALU.is_gt, fill=MASKED,
                                    base=(BLOCKS - 1) * P, pattern=[[-1, S + 7 * P]],
                                    channel_multiplier=1).then_inc(consts_set, 1)

            def take(b):
                pool.wait_ge(picks_ready, b + 1)
                apart(pool)
                nc.gpsimd.tensor_copy(idx_mix[:], idx_next[:]).then_inc(idx_taken, 1)
                pool.wait_ge(idx_taken, b + 1)
                apart(pool)

            def two_rounds(b, m):
                for r in range(2):
                    first = m * 2 * V_SLOTS + r * V_SLOTS
                    nc.gpsimd.tensor_copy(idx_now[:, r, :], idx_mix[:, bass.ds(first, V_SLOTS)]).then_inc(idx_slice, 1)
                    pool.wait_ge(idx_slice, (b * (PICKS // V_SLOTS)) + 2 * m + r + 1)
                    apart(pool)
                    for g in range(V_SLOTS // GROUP):
                        n = b * GROUPS + (2 * m + r) * (V_SLOTS // GROUP) + g
                        wait(pool, dots_done, n + 1 - U_SLOTS // GROUP)
                        apart(pool)
                        for j in range(g * GROUP, (g + 1) * GROUP):
                            nc.gpsimd.indirect_dma_start(
                                out=u_ring[:, j % U_SLOTS, :], out_offset=None, in_=peer_u,
                                in_offset=bass.IndirectOffsetOnAxis(ap=idx_now[:, r, j:j + 1], axis=0),
                            ).then_inc(u_in[j % U_SLOTS], 16)
                        wait(pool, group_done, n + 1 - V_SLOTS // GROUP)
                        apart(pool)
                        for j in range(g * GROUP, (g + 1) * GROUP):
                            nc.gpsimd.indirect_dma_start(
                                out=v_ring[:, j, :], out_offset=None, in_=peer_v,
                                in_offset=bass.IndirectOffsetOnAxis(ap=idx_now[:, r, j:j + 1], axis=0),
                            ).then_inc(v_in[j], 16)

            rounds = PICKS // (2 * V_SLOTS)
            take(0)
            two_rounds(0, 0)
            with pool.Fori(1, rounds) as m:
                two_rounds(0, m)
            with pool.Fori(1, BLOCKS) as b:
                take(b)
                with pool.Fori(0, rounds) as m:
                    two_rounds(b, m)

        @block.tensor
        def _(pe):
            def piece(b, j):
                pe.wait_ge(w_in[j % W_SLOTS], 16 * (b * (PIECES // W_SLOTS) + j // W_SLOTS + 1))
                return w_ring[:, j % W_SLOTS, :]

            def product(b, j):
                w = piece(b, j)
                if j < PIECE_XC:
                    o = (pm[:, 0:512], pm[:, 512:1024], pz[:, 0:512])[j // 4]
                    terms = [(o, hT[:, k, :], w[:, (k % 2) * 512:(k % 2 + 1) * 512], k == 0, k == KD - 1)
                             for k in (2 * (j % 4), 2 * (j % 4) + 1)]
                elif PIECE_OUT <= j < PIECE_PEER:
                    o, half = (pm, pz)[(j - PIECE_OUT) // 4], (j % 4) // 2
                    src = (sbT, cvT)[half]
                    terms = [(o[:, half * 512:(half + 1) * 512], src[:, c, :],
                              w[:, (c % 2) * 512:(c % 2 + 1) * 512], c == 0, c == CH - 1)
                             for c in (2 * (j % 2), 2 * (j % 2) + 1)]
                else:
                    q = (j - PIECE_PEER) // 4
                    bank = 0 if j < PIECE_OUT else (q % 2) * 512
                    o = pm[:, bank + (j % 4) * P:bank + (j % 4 + 1) * P]
                    terms = [(o, w[:, k * P:(k + 1) * P], hT[:, k, :], k == 0, k == KD - 1) for k in range(KD)]
                for o, left, right, start, stop in terms:
                    mm = nc.tensor.matmul(o, left, right, start=start, stop=stop)
                mm.then_inc(piece_done, 1)

            def turn(dst, src, tiles):
                for t in range(tiles):
                    mm = nc.tensor.transpose(dst[:, t * P:(t + 1) * P], src[:, t * P:(t + 1) * P], ident[:])
                return mm

            def scores(b, i):
                if i == 0:
                    pe.wait_ge(v_kept, b + 1)
                    pe.wait_ge(qkT_ready, 2 * b + 2)
                wait(pe, z_masked, b * HEADS + i)
                r = DH * (i % 2)
                for half in range(2):
                    mm = nc.tensor.matmul(pz[:, half * 512:(half + 1) * 512], qT[r:r + DH, i // 2, :],
                                          kT[r:r + DH, i // 2, half * 512:(half + 1) * 512],
                                          start=True, stop=True)
                mm.then_inc(z_psum, 1)

            def values(b, h):
                pe.wait_ge(aT_ready, b * HEADS + h + 1)
                for t in range(BLOCKS):
                    mm = nc.tensor.matmul(po[:, h * DH:(h + 1) * DH], rd[:, t * P:(t + 1) * P],
                                          vals_sb[:, t, h * DH:(h + 1) * DH],
                                          start=(t == 0), stop=(t == BLOCKS - 1))
                mm.then_inc(av_done, 1)

            def peer_scores(b, q):
                pe.wait_ge(pq_ready, 4 * b + q + 1)
                if q >= 2:
                    pe.wait_ge(s_ready, 4 * b + q - 1)
                o = (q % 2) * 512
                for c in range(4):
                    mm = nc.tensor.matmul(pz[:, o + c * P:o + (c + 1) * P], rd[:, o + c * P:o + (c + 1) * P],
                                          keysT[:, (c % 2) * NKEYS:(c % 2 + 1) * NKEYS],
                                          start=True, stop=True)
                mm.then_inc(s_psum, 1)

            def early(b, t):
                if t == S_QK + 1:
                    pe.wait_ge(qk_norm, 2 * b + 2)
                    turn(pt, rb, 8).then_inc(qk_turned, 1)
                if S_HEAD < t <= S_HEAD + HEADS:
                    h = t - S_HEAD - 1
                    pe.wait_ge(a_ready, b * HEADS + h + 1)
                    if h >= 1:
                        pe.wait_ge(aT_ready, b * HEADS + h)
                    turn(pt, rb, BLOCKS).then_inc(a_turned, 1)

            def late(b, t):
                if t == S_NORM1 + 1:
                    pe.wait_ge(h_ready, b + 1)
                    wait(pe, h2T_ready, b)
                    turn(pt, ra, KD).then_inc(h_turned, 1)
                if S_HEAD < t <= S_HEAD + HEADS:
                    values(b, t - S_HEAD - 1)
                if S_HEAD - 1 <= t < S_HEAD - 1 + HEADS:
                    scores(b, t - S_HEAD + 1)
                if t == S_CONV + 6:
                    pe.wait_ge(cv_sq, b + 1)
                    for c in range(CH):
                        mm = nc.tensor.matmul(pm[:, 0:1], h_next[:, 512 + c * P:512 + (c + 1) * P], ones[:],
                                              start=(c == 0), stop=(c == CH - 1))
                    mm.then_inc(cv_ss, 1)
                if t == S_SB:
                    pe.wait_ge(sb_kept, b + 1)
                    turn(pt, rd, CH).then_inc(sb_turned, 1)
                if t == S_NORM2:
                    pe.wait_ge(h2_ready, b + 1)
                    turn(pt, h_next, KD).then_inc(h2_turned, 1)
                if t == S_PROJ:
                    pe.wait_ge(hT_ready, b + 1)
                    wait(pe, s_ready, b * 4)
                if t == S_CONV + 2:
                    pe.wait_ge(xc_kept, b + 1)
                if t == S_CONV + 4:
                    pe.wait_ge(u_ready, b + 1)
                if t == S_OUT:
                    pe.wait_ge(sbT_ready, b + 1)
                    pe.wait_ge(cvT_ready, b + 1)
                    pe.wait_ge(cv_ss_kept, b + 1)
                if t == S_PEER:
                    pe.wait_ge(h2T_ready, b + 1)
                for j in range(*PIECES_AT.get(t, (0, 0))):
                    if j in (PIECE_PEER + 8, PIECE_PEER + 12):
                        pe.wait_ge(pq_ready, 4 * b + (j - PIECE_PEER) // 4 - 1)
                    product(b, j)
                if S_PEER + 2 <= t < S_PEER + 6:
                    peer_scores(b, t - S_PEER - 2)

            def mix(b, n):
                pe.wait_ge(diag_ready, b * GROUPS + n + 1)
                if n == 0:
                    pe.wait_ge(acc_free, b + 1)
                for j in range(GROUP):
                    k = n * GROUP + j
                    pe.wait_ge(v_in[k % V_SLOTS], 16 * (b * (PICKS // V_SLOTS) + k // V_SLOTS + 1))
                    for half in range(2):
                        mm = nc.tensor.matmul(acc[:, half * 512:(half + 1) * 512], diag[:, n % 2, j, :],
                                              v_ring[:, k % V_SLOTS, half * 512:(half + 1) * 512],
                                              start=(k == 0), stop=(k == PICKS - 1))
                mm.then_inc(group_done, 1)

            pe.wait_ge(consts_in, 48)
            pe.wait_ge(consts_set, 5)
            for t in range(S_LAST + 1):
                early(0, t)
                late(0, t)
            with pe.Fori(1, BLOCKS) as b:
                for t in range(GROUPS):
                    early(b, t)
                    if t >= 1:
                        mix(b - 1, t - 1)
                    late(b, t)
                mix(b - 1, GROUPS - 1)
            for n in range(GROUPS):
                mix(BLOCKS - 1, n)

        @block.scalar
        def _(act):
            copy = ACT.Copy

            def front(b, t):
                if t == S_NORM1 + 1:
                    act.wait_ge(norm1, b + 1)
                    nc.scalar.activation(ra[:, 0:D], rb[:], copy, scale=inv1[:]).then_inc(h_ready, 1)
                if t == S_QK:
                    act.wait_ge(piece_done, b * PIECES + PIECE_K + 4)
                    for i in range(2):
                        nc.scalar.activation(rc[:, i * 512:(i + 1) * 512], pm[:, i * 512:(i + 1) * 512],
                                             ACT.Square).then_inc(qk_sq, 1)
                if t == S_QK + 1:
                    act.wait_ge(qk_turned, b + 1)
                    nc.scalar.activation(qT[:], grid(pt[:, 0:512], CH), copy,
                                         scale=chan_sb[:, C_GQ:C_GQ + 1]).then_inc(qkT_ready, 1)
                    nc.scalar.activation(kT[:, :, bass.ds(b * P, P)], grid(pt[:, 512:1024], CH), copy,
                                         scale=chan_sb[:, C_GK:C_GK + 1]).then_inc(qkT_ready, 1)
                    act.wait_ge(piece_done, b * PIECES + PIECE_V + 4)
                    nc.scalar.activation(vals_sb[:, bass.ds(b, 1), :], pz[:, 0:512].unsqueeze(1),
                                         copy).then_inc(v_kept, 1)
                if t == S_CONV + 2:
                    act.wait_ge(piece_done, b * PIECES + PIECE_XC + 4)
                    nc.scalar.activation(h_next[:, 0:512], pm[:, 0:512], copy).then_inc(xc_kept, 1)
                if t == S_CONV + 6:
                    act.wait_ge(cv_raw, b + 1)
                    nc.scalar.activation(h_next[:, 512:1024], h_next[:, 0:512], ACT.Square).then_inc(cv_sq, 1)
                if S_HEAD < t <= S_HEAD + HEADS:
                    h = t - S_HEAD - 1
                    act.wait_ge(a_turned, b * HEADS + h + 1)
                    wait(act, av_done, b * HEADS + h)
                    if h == 0:
                        wait(act, s_psum, 4 * b)
                    nc.scalar.activation(rd[:], pt[:], copy).then_inc(aT_ready, 1)
                if S_HEAD <= t < S_HEAD + HEADS:
                    i = t - S_HEAD
                    act.wait_ge(z_masked, b * HEADS + i + 1)
                    nc.scalar.activation(rb[:], ra[:, 0:S], ACT.Sigmoid, scale=SCALE)
                    nc.scalar.activation(rc[:], ra[:, 0:S], ACT.Sigmoid, scale=-SCALE).then_inc(beta_ready, 1)
                if t == S_SB:
                    act.wait_ge(av_done, (b + 1) * HEADS)
                    nc.scalar.activation(rd[:, 0:512], po, copy).then_inc(sb_kept, 1)
                if t == S_NORM2 + 1:
                    act.wait_ge(h2_turned, b + 1)
                    nc.scalar.activation(hT[:], grid(pt[:], KD), copy).then_inc(h2T_ready, 1)
                if S_RANK <= t < S_RANK + 4:
                    q, o = t - S_RANK, ((t - S_RANK) % 2) * 512
                    act.wait_ge(s_psum, 4 * b + q + 1)
                    if q >= 2:
                        act.wait_ge(s_ranked, 4 * b + q - 1)
                    nc.scalar.activation(rb[:, o:o + 512], pz[:, o:o + 512], copy).then_inc(s_ready, 1)
                if S_PEER + 2 <= t < S_PEER + 6:
                    q, o = t - S_PEER - 2, ((t - S_PEER - 2) % 2) * 512
                    act.wait_ge(piece_done, b * PIECES + PIECE_PEER + 4 * (q + 1))
                    if q == 0:
                        act.wait_ge(sb_turned, b + 1)
                    nc.scalar.activation(rd[:, o:o + 512], pm[:, o:o + 512], copy).then_inc(pq_ready, 1)
                if t == S_LAST:
                    act.wait_ge(gate_arg, b + 1)
                    nc.scalar.activation(gate_e[:], gate_e[:], ACT.Exp).then_inc(gate_exp, 1)

            def diagonals(b, n):
                act.wait_ge(wgt_ready, b * GROUPS + n + 1)
                if n == 0:
                    act.wait_ge(acc_free, b + 1)
                else:
                    wait(act, group_done, b * GROUPS + n - 1)
                for j in range(GROUP):
                    a = nc.scalar.activation(diag[:, n % 2, j, :], ident[:], copy, scale=wgt[:, n % 2, j:j + 1])
                a.then_inc(diag_ready, 1)

            def gelu(b, n):
                act.wait_ge(dots_done, b * GROUPS + n + 1)
                nc.scalar.activation(acts[:, n % 2, :], dots[:, n % 2, :], ACT.Gelu).then_inc(gelu_done, 1)

            def take(b):
                act.wait_ge(picks_ready, b + 1)
                nc.scalar.activation(h_mix[:], h_next[:], copy).then_inc(h_mix_set, 1)
                nc.scalar.activation(gate_mix[:], gate_next[:].rearrange("p h k -> p (h k)"),
                                     copy).then_inc(h_mix_set, 1)

            def take_residual(b):
                act.wait_ge(x_mix_free, b + 1)
                nc.scalar.activation(x_mix[:], x_next[:], copy).then_inc(x_mix_set, 1)

            act.wait_ge(consts_in, 48)
            act.wait_ge(consts_set, 5)
            for t in range(S_LAST + 1):
                front(0, t)
            with act.Fori(1, BLOCKS) as b:
                take(b - 1)
                for t in range(GROUPS):
                    if t >= 1:
                        diagonals(b - 1, t - 1)
                    front(b, t)
                    gelu(b - 1, t)
                    if t == 1:
                        take_residual(b - 1)
                diagonals(b - 1, GROUPS - 1)
            take(BLOCKS - 1)
            for n in range(GROUPS):
                if n >= 1:
                    diagonals(BLOCKS - 1, n - 1)
                gelu(BLOCKS - 1, n)
                if n == 1:
                    take_residual(BLOCKS - 1)
            diagonals(BLOCKS - 1, GROUPS - 1)

        @block.vector
        def _(dve):
            V = nc.vector
            count = {"here": 0, "front": 0}

            def step(ins):
                ins.then_inc(own_v, 1)
                count["here"] += 1

            def settle(b):
                dve.wait_ge(own_v, b * count["front"] + count["here"])

            def inverse_root(b, o, sums, n, scale, done=None):
                a, t = rs_a[:, 0:n], rs_t[:, 0:n]
                step(V.tensor_scalar(a, sums, scale, EPS, ALU.mult, ALU.add))
                settle(b)
                step(V.tensor_scalar(o.bitcast(I32), a.bitcast(I32), 1, None, ALU.logical_shift_right))
                settle(b)
                step(V.tensor_scalar(o.bitcast(I32), o.bitcast(I32), -1.0, MAGIC, ALU.mult, ALU.add))
                settle(b)
                for i in range(4):
                    step(V.tensor_tensor(t, o, o, ALU.mult))
                    settle(b)
                    step(V.scalar_tensor_tensor(t, t, -0.5, a, ALU.mult, ALU.mult))
                    settle(b)
                    last = V.scalar_tensor_tensor(o, t, 1.5, o, ALU.add, ALU.mult)
                    if i == 3 and done is not None:
                        last.then_inc(done, 1)
                    else:
                        step(last)
                        settle(b)

            def square_sum(b, src, junk, o):
                step(V.tensor_tensor_reduce(junk, src, src, 1.0, 0.0, ALU.mult, ALU.add, o))

            def mask(b, i):
                dve.wait_ge(z_psum, b * HEADS + i + 1)
                if i >= 1:
                    dve.wait_ge(a_ready, b * HEADS + i)
                apart(dve)
                V.tensor_tensor(ra[:, 0:S], pz[:], band[:, bass.ds((BLOCKS - 1 - b) * P, S)],
                                ALU.add).then_inc(z_masked, 1)

            def stick(b, i):
                dve.wait_ge(beta_ready, b * HEADS + i + 1)
                step(V.tensor_tensor_scan(ra[:, 0:S][:, ::-1], rc[:, ::-1], rc[:, ::-1], 1.0,
                                          ALU.mult, ALU.bypass))
                settle(b)
                V.tensor_tensor(rb[:], rb[:], ra[:, 1:S + 1], ALU.mult).then_inc(a_ready, 1)

            def rank(b, q):
                dve.wait_ge(s_ready, 4 * b + q + 1)
                o = (q % 2) * 512
                apart(dve)
                row = lambda r, c: r[:, o + c * NKEYS:o + (c + 1) * NKEYS]
                for c in range(4):
                    step(V.max(top_v[:, 4 * q + c, 0:8], row(rb, c)))
                settle(b)
                apart(dve)
                for c in range(4):
                    step(V.max_index(top_i[:, 4 * q + c, 0:8], top_v[:, 4 * q + c, 0:8], row(rb, c)))
                for c in range(4):
                    step(V.match_replace(row(rc, c), top_v[:, 4 * q + c, 0:8], row(rb, c), TAKEN))
                settle(b)
                apart(dve)
                for c in range(4):
                    step(V.max(top_v[:, 4 * q + c, 8:16], row(rc, c)))
                settle(b)
                apart(dve)
                for c in range(4):
                    i = V.max_index(top_i[:, 4 * q + c, 8:16], top_v[:, 4 * q + c, 8:16], row(rc, c))
                i.then_inc(s_ranked, 1)

            def combine(b, q):
                dve.wait_ge(s_ranked, 4 * b + 3 + q)
                h0 = 4 * q
                first = top_v[:, 2 * h0:2 * h0 + 8:2, :].unsqueeze(3).to_broadcast([P, 4, TOPK, TOPK])
                second = top_v[:, 2 * h0 + 1:2 * h0 + 8:2, :].unsqueeze(2).to_broadcast([P, 4, TOPK, TOPK])
                step(V.tensor_tensor(rc[:].rearrange("p (h i j) -> p h i j", h=4, i=TOPK), first, second, ALU.add))
                settle(b)
                apart(dve)
                row = lambda r, c: r[:, c * 256:(c + 1) * 256]
                for c in range(4):
                    step(V.max(sum_v[:, h0 + c, 0:8], row(rc, c)))
                settle(b)
                apart(dve)
                for c in range(4):
                    step(V.max_index(sum_p[:, h0 + c, 0:8], sum_v[:, h0 + c, 0:8], row(rc, c)))
                for c in range(4):
                    step(V.match_replace(row(ra, c), sum_v[:, h0 + c, 0:8], row(rc, c), TAKEN))
                settle(b)
                apart(dve)
                for c in range(4):
                    step(V.max(sum_v[:, h0 + c, 8:16], row(ra, c)))
                settle(b)
                apart(dve)
                for c in range(4):
                    step(V.max_index(sum_p[:, h0 + c, 8:16], sum_v[:, h0 + c, 8:16], row(ra, c)))
                settle(b)

            def look_up(b, q):
                if q == 0:
                    flat = sum_p[:].rearrange("p h k -> p (h k)")
                    step(V.tensor_scalar(pos[:, 0, :], flat, 4, None, ALU.logical_shift_right))
                    step(V.tensor_scalar(pos[:, 1, :], flat, 15, None, ALU.bitwise_and))
                    step(V.tensor_copy(top_f[:], top_i[:]))
                    settle(b)
                    step(V.tensor_copy(pos_f[:], pos[:]))
                    settle(b)
                k0 = q * 64
                for half, r in ((0, ra), (1, rc)):
                    hot = r[:, 0:1024].rearrange("p (k a) -> p k a", a=TOPK)
                    step(V.tensor_tensor(hot, iota_f[:].unsqueeze(1).to_broadcast([P, 64, TOPK]),
                                         spread(pos_f[:, half, k0:k0 + 64], TOPK), ALU.is_equal))
                settle(b)
                for half, r in ((0, ra), (1, rc)):
                    hot = r[:, 0:1024].rearrange("p (h k a) -> p h k a", h=4, a=TOPK)
                    step(V.tensor_tensor(hot, hot, top_f[:, 8 * q + half:8 * q + 8:2, :].unsqueeze(2)
                                         .to_broadcast([P, 4, TOPK, TOPK]), ALU.mult))
                settle(b)
                for half, r in ((0, ra), (1, rc)):
                    hot = r[:, 0:1024].rearrange("p (k a) -> p k a", a=TOPK)
                    step(V.tensor_reduce(sel[:, half, k0:k0 + 64], hot, AX_X, ALU.add))
                settle(b)

            def early(b, t):
                if t == S_NORM1:
                    dve.wait_ge(x_in, 16 * (b + 1))
                    square_sum(b, rb[:], ra[:, 0:D], ss[:, 0:1])
                    settle(b)
                    inverse_root(b, inv1[:], ss[:, 0:1], 1, 1.0 / D, done=norm1)
                if t == S_PROJ:
                    dve.wait_ge(h_turned, b + 1)
                    V.tensor_tensor(hT[:], grid(pt[:], KD), spread(chan_sb[:, C_G1:C_G1 + KD], P),
                                    ALU.mult).then_inc(hT_ready, 1)
                if S_HEAD <= t < S_HEAD + HEADS:
                    mask(b, t - S_HEAD)
                if t == S_CONV + 4:
                    step(V.tensor_copy(uT[:, :, 0:2], uT[:, :, P:P + 2]))
                    settle(b)
                    dve.wait_ge(xc_kept, b + 1)
                    dve.wait_ge(piece_done, b * PIECES + PIECE_C + 4)
                    V.tensor_tensor(uT[:, :, 2:P + 2], grid(pm[:, 0:512], CH), grid(h_next[:, 0:512], CH),
                                    ALU.mult).then_inc(u_ready, 1)
                if t == S_CONV + 6:
                    dve.wait_ge(piece_done, b * PIECES + PIECE_B + 4)
                    V.tensor_tensor(grid(h_next[:, 0:512], CH), grid(pm[:, 0:512], CH),
                                    grid(h_next[:, 512:1024], CH), ALU.mult).then_inc(cv_raw, 1)
                    dve.wait_ge(cv_raw, b + 1)
                    V.tensor_tensor(cvT[:], grid(h_next[:, 0:512], CH), spread(chan_sb[:, C_GCV:C_GCV + CH], P),
                                    ALU.mult).then_inc(cvT_ready, 1)
                if t == S_CONV + 7:
                    dve.wait_ge(cv_ss, b + 1)
                    V.tensor_copy(ss2[:, 1:2], pm[:, 0:1]).then_inc(cv_ss_kept, 1)
                if t == S_OUT:
                    dve.wait_ge(sb_turned, b + 1)
                    V.tensor_tensor(sbT[:], grid(pt[:, 0:512], CH), spread(chan_sb[:, C_GSB:C_GSB + CH], P),
                                    ALU.mult).then_inc(sbT_ready, 1)
                if t == S_NORM2:
                    dve.wait_ge(residual_in, 16 * (b + 1))
                    for i in range(2):
                        for n, o in enumerate((pm, pz)):
                            if i == 0:
                                dve.wait_ge(piece_done, b * PIECES + PIECE_OUT + 4 * (n + 1))
                            xs = x_next[:, n * 512:(n + 1) * 512]
                            step(V.scalar_tensor_tensor(xs, o[:, i * 512:(i + 1) * 512], inv2[:, i:i + 1], xs,
                                                        ALU.mult, ALU.add))
                        settle(b)
                    square_sum(b, x_next[:], ra[:, 0:D], ss[:, 0:1])
                    settle(b)
                    inverse_root(b, invh[:], ss[:, 0:1], 1, 1.0 / D)
                    V.scalar_tensor_tensor(h_next[:], x_next[:], invh[:], g2_all[:], ALU.mult,
                                           ALU.mult).then_inc(h2_ready, 1)
                if t in (S_JOIN, S_JOIN + 1):
                    combine(b, t - S_JOIN)
                if t == S_JOIN + 1:
                    V.tensor_tensor(gate_e[:], sum_v[:], sum_v[:, :, 0:1].to_broadcast([P, PH, TOPK]),
                                    ALU.subtract).then_inc(gate_arg, 1)
                if t == S_LAST:
                    look_up(b, 1)

            def late(b, t):
                if t == S_QK:
                    dve.wait_ge(qk_sq, 2 * (b + 1))
                    step(V.tensor_reduce(ss[:], grid(rc[:], 2 * HEADS), AX_X, ALU.add))
                    settle(b)
                    inverse_root(b, invqk[:], ss[:], 2 * HEADS, 1.0 / DH)
                    for i in range(2):
                        V.tensor_tensor(grid(rb[:, i * 512:(i + 1) * 512], HEADS),
                                        grid(pm[:, i * 512:(i + 1) * 512], HEADS),
                                        spread(invqk[:, i * HEADS:(i + 1) * HEADS], DH),
                                        ALU.mult).then_inc(qk_norm, 1)
                if S_HEAD <= t < S_HEAD + HEADS:
                    stick(b, t - S_HEAD)
                if t == S_CONV + 4:
                    y = grid(h_next[:, 512:1024], CH)
                    tap = lambda w, c: chan_sb[:, C_CONV + w * CH + c:C_CONV + w * CH + c + 1]
                    dve.wait_ge(u_ready, b + 1)
                    for c in range(CH):
                        step(V.tensor_scalar(y[:, c, :], uT[:, c, 0:P], tap(0, c), None, ALU.mult))
                    for w in (1, 2):
                        settle(b)
                        for c in range(CH):
                            step(V.scalar_tensor_tensor(y[:, c, :], uT[:, c, w:w + P], tap(w, c), y[:, c, :],
                                                        ALU.mult, ALU.add))
                    settle(b)
                if t == S_SB:
                    dve.wait_ge(sb_kept, b + 1)
                    square_sum(b, rd[:, 0:512], rb[:, 0:512], ss2[:, 0:1])
                    settle(b)
                    inverse_root(b, inv2[:], ss2[:], 2, 1.0 / DSB)
                if S_RANK <= t < S_RANK + 4:
                    rank(b, t - S_RANK)
                if t == S_JOIN + 1:
                    look_up(b, 0)
                if t == S_LAST:
                    dve.wait_ge(gate_exp, b + 1)
                    step(V.tensor_reduce(den[:], gate_e[:], AX_X, ALU.add))
                    settle(b)
                    step(V.reciprocal(rden[:], den[:]))
                    settle(b)
                    wait(dve, h_mix_set, 2 * b)
                    step(V.tensor_tensor(gate_next[:], gate_e[:], spread(rden[:], TOPK), ALU.mult))
                    wait(dve, idx_taken, b)
                    V.scalar_tensor_tensor(idx_next[:], sel[:, 0, :], float(NKEYS), sel[:, 1, :], ALU.mult,
                                           ALU.add).then_inc(picks_ready, 1)

            def weights(b, n):
                dve.wait_ge(gelu_done, b * GROUPS + n + 1)
                V.tensor_tensor(wgt[:, n % 2, :], acts[:, n % 2, :], gate_mix[:, n * GROUP:(n + 1) * GROUP],
                                ALU.mult).then_inc(wgt_ready, 1)

            def dot(b, n):
                for j in range(GROUP):
                    k = n * GROUP + j
                    dve.wait_ge(u_in[k % U_SLOTS], 16 * (b * (PICKS // U_SLOTS) + k // U_SLOTS + 1))
                    u = u_ring[:, k % U_SLOTS, :]
                    d = V.tensor_tensor_reduce(u, u, h_mix[:], 1.0, 0.0, ALU.mult, ALU.add,
                                               dots[:, n % 2, j:j + 1])
                d.then_inc(dots_done, 1)

            def finish(b):
                dve.wait_ge(group_done, (b + 1) * GROUPS)
                dve.wait_ge(x_mix_set, b + 1)
                V.tensor_tensor(x_mix[:], acc[:], x_mix[:], ALU.add).then_inc(acc_free, 1)

            dve.sem_inc(acc_free, 1)
            step(V.memset(ra[:, S:S + 1], 1.0))
            step(V.memset(uT[:], 0.0))
            step(V.memset(kT[:], 0.0))
            step(V.memset(vals_sb[:], 0.0))
            dve.wait_ge(iota_set, 1)
            step(V.tensor_copy(iota_f[:], iota_i[:]))
            settle(0)
            set_up = count["here"]
            dve.wait_ge(consts_in, 48)
            dve.wait_ge(consts_set, 5)
            for t in range(S_LAST + 1):
                early(0, t)
                late(0, t)
            count["front"] = count["here"] - set_up
            with dve.Fori(1, BLOCKS) as b:
                count["here"] = set_up
                dve.wait_ge(h_mix_set, 2 * b)
                for t in range(GROUPS):
                    if t >= 1:
                        weights(b - 1, t - 1)
                    early(b, t)
                    dot(b - 1, t)
                    late(b, t)
                weights(b - 1, GROUPS - 1)
                finish(b - 1)
            dve.wait_ge(h_mix_set, 2 * BLOCKS)
            for n in range(GROUPS):
                if n >= 1:
                    weights(BLOCKS - 1, n - 1)
                dot(BLOCKS - 1, n)
            weights(BLOCKS - 1, GROUPS - 1)
            finish(BLOCKS - 1)


def kernel(x, norm1_g, w_in, q_norm_g, k_norm_g, conv_w, sb_out_g, conv_out_g, w_out, norm2_g, peer_w_q,
           peer_sub_keys, peer_u, peer_v):
    import numpy as np
    import concourse.bacc as bacc
    from concourse.bass_utils import run_bass_kernel_spmd

    def by_rows(w):
        n = w.shape[1] // 512
        w = w.reshape(4, 2, P, n, 512).transpose(3, 0, 2, 1, 4)
        return w.reshape(4 * n, P, 1024)

    def by_columns(w):
        n = w.shape[1] // P
        return w.reshape(KD, P, n, P).transpose(2, 1, 0, 3).reshape(n, P, 1024)

    a = {k: np.asarray(v)[0] for k, v in dict(
        x=x, norm1_g=norm1_g, w_in=w_in, q_norm_g=q_norm_g, k_norm_g=k_norm_g, conv_w=conv_w, sb_out_g=sb_out_g,
        conv_out_g=conv_out_g, w_out=w_out, peer_w_q=peer_w_q, peer_sub_keys=peer_sub_keys, peer_u=peer_u,
        peer_v=peer_v).items()}
    part = [a["w_in"][:, i * DSB:(i + 1) * DSB] for i in range(6)]
    wstream = np.concatenate([by_rows(part[0]), by_rows(part[1]), by_rows(part[2]), by_columns(part[3]),
                              by_columns(part[5]), by_columns(part[4]), by_rows(a["w_out"]),
                              by_columns(a["peer_w_q"])])
    chan = np.concatenate([
        a["norm1_g"].reshape(KD, P).T, a["conv_w"].reshape(3, CH, P).transpose(2, 0, 1).reshape(P, 3 * CH),
        a["conv_out_g"].reshape(CH, P).T, a["sb_out_g"].reshape(CH, P).T,
        np.concatenate([a["q_norm_g"]] * 2)[:, None], np.concatenate([a["k_norm_g"]] * 2)[:, None]], axis=1)
    arrays = {
        "x_in_dram": a["x"], "wstream": wstream, "chan": chan,
        "keys": a["peer_sub_keys"].transpose(2, 0, 1).reshape(P, 2 * NKEYS), "norm2": np.asarray(norm2_g),
        "table_u": a["peer_u"], "table_v": a["peer_v"],
    }
    arrays = {k: np.ascontiguousarray(v) for k, v in arrays.items()}
    nc = bacc.Bacc("TRN2", target_bir_lowering=False, num_devices=1)
    ins = [nc.dram_tensor(k, v.shape, F32, kind="ExternalInput").ap() for k, v in arrays.items()]
    out = nc.dram_tensor("y_out_dram", (S, D), F32, kind="ExternalOutput").ap()
    build(nc, *ins, out)
    r = run_bass_kernel_spmd(nc, [arrays], core_ids=[0])
    return r.results[0]["y_out_dram"].reshape(1, S, D)
```

```python
from contextlib import ExitStack

import concourse.bass as bass
from concourse import mybir

F32 = mybir.dt.float32
BF16 = mybir.dt.bfloat16
U32 = mybir.dt.uint32
I32 = mybir.dt.int32
ALU = mybir.AluOpType
ACT = mybir.ActivationFunctionType
AX_X = mybir.AxisListType.X

P = 128
D = 1024
S = 1024
BLOCKS = S // P
KD = D // P
HEADS = 8
DH = 64
DSB = HEADS * DH
CH = DSB // P
SCALE = DH ** -0.5
PH = 8
TOPK = 16
NKEYS = 128
PICKS = PH * TOPK
GROUP = 4
GROUPS = PICKS // GROUP
U_SLOTS = 8
V_SLOTS = 16
W_SLOTS = 4
PIECES = 48
PIECE_Q, PIECE_K, PIECE_V, PIECE_XC, PIECE_C, PIECE_B, PIECE_OUT, PIECE_PEER = 0, 4, 8, 12, 16, 20, 24, 32
EPS = 1e-6
MASKED = -1e30
TAKEN = -3e38
MAGIC = float(0x5F3759DF)
S_NORM1 = 0
S_PROJ = 2
S_QK = 4
S_CONV = 5
S_HEAD = 6
S_CONV_OUT = 14
S_SB = 15
S_OUT = 16
S_NORM2 = 17
S_PEER = 18
S_RANK = 20
S_JOIN = {22: 0, 24: 1, 25: 2, 26: 3}
S_LOOK = {24: 0, 26: 1, 27: 2, 28: 3}
S_JOIN_FIRST = {21: 0, 24: 1, 25: 2, 26: 3}
S_LOOK_FIRST = {21: 0, 25: 1, 27: 2, 28: 3}
S_DOTS_FIRST = {24: 0, 26: 1}
S_LAST = 28
PIECES_AT = {**{S_PROJ + i: (4 * i, 4 * i + 4) for i in range(3)},
             **{S_CONV + i: (12 + 2 * i, 14 + 2 * i) for i in range(6)},
             **{S_CONV_OUT + i: (24 + 2 * i, 26 + 2 * i) for i in range(2)}, S_OUT: (28, 32),
             **{S_PEER + i: (32 + 4 * i, 36 + 4 * i) for i in range(4)}}
C_G1, C_CONV, C_GCV, C_GSB, C_GQ, C_GK, C_END = 0, 8, 20, 24, 28, 29, 30


def build(nc, x, wstream, chan, keys, norm2_g, peer_u, peer_v, out):
    with ExitStack() as ctx:
        def sb(name, shape, dt=F32):
            return ctx.enter_context(nc.sbuf_tensor(name, shape, dt))

        def ps(name, shape):
            return ctx.enter_context(nc.psum_tensor(name, shape, F32))

        def sem(name):
            return ctx.enter_context(nc.semaphore(name))

        u_ring = sb("u_ring", [P, U_SLOTS, D])
        v_ring = sb("v_ring", [P, V_SLOTS, D])
        w_ring = sb("w_ring", [P, W_SLOTS, 1024])
        kT = sb("kT", [P, CH, S])
        vals_sb = sb("vals_sb", [P, BLOCKS, DSB])
        x_next = sb("x_next", [P, D])
        x_mix = sb("x_mix", [P, D])
        h_next = sb("h_next", [P, D])
        h_mix = sb("h_mix", [P, D])
        hT = sb("hT", [P, KD, P])
        g2_all = sb("g2_all", [P, D])
        ra = sb("ra", [P, S])
        rb = sb("rb", [P, S])
        rc = sb("rc", [P, S])
        rd = sb("rd", [P, S])
        band = sb("band", [P, S + 7 * P], BF16)
        qT = sb("qT", [P, CH, P])
        uT = sb("uT", [P, CH, P + 2])
        cvT = sb("cvT", [P, CH, P])
        sbT = sb("sbT", [P, CH, P])
        diag = sb("diag", [P, 2, GROUP, P])
        keysT = sb("keysT", [P, 2 * NKEYS])
        ident = sb("ident", [P, P])
        ones = sb("ones", [P, 1])
        chan_sb = sb("chan_sb", [P, C_END])
        iota_i = sb("iota_i", [P, TOPK], I32)
        iota_f = sb("iota_f", [P, TOPK])
        top_v = sb("top_v", [P, 2 * PH, TOPK])
        top_i = sb("top_i", [P, 2 * PH, TOPK], U32)
        sum_v = sb("sum_v", [P, PH, TOPK])
        sum_p = sb("sum_p", [P, PH, TOPK], U32)
        sb_flat, cv_flat = (a[:].rearrange("p c t -> p (c t)") for a in (sbT, cvT))
        top_f = sb_flat[:, 0:256].rearrange("p (c k) -> p c k", c=2 * PH)
        pos = sb_flat[:, 256:512].bitcast(U32).rearrange("p (i k) -> p i k", i=2)
        pos_f = cv_flat[:, 0:256].rearrange("p (i k) -> p i k", i=2)
        sel = cv_flat[:, 256:512].rearrange("p (i k) -> p i k", i=2)
        gate_e = sb("gate_e", [P, PH, TOPK])
        gate_next = sb("gate_next", [P, PH, TOPK])
        gate_mix = sb("gate_mix", [P, PICKS])
        den = sb("den", [P, PH])
        rden = sb("rden", [P, PH])
        idx_next = sb("idx_next", [P, PICKS], U32)
        idx_mix = sb("idx_mix", [P, PICKS], U32)
        idx_now = sb("idx_now", [P, 2, V_SLOTS], U32)
        ss = sb("ss", [P, 2 * HEADS])
        rs_a = sb("rs_a", [P, 2 * HEADS])
        rs_t = sb("rs_t", [P, 2 * HEADS])
        inv1 = sb("inv1", [P, 1])
        invqk = sb("invqk", [P, 2 * HEADS])
        ss2 = sb("ss2", [P, 2])
        inv2 = sb("inv2", [P, 2])
        invh = sb("invh", [P, 1])
        dots = sb("dots", [P, 2, GROUP])
        acts = sb("acts", [P, 2, GROUP])
        wgt = sb("wgt", [P, 2, GROUP])

        acc = ps("acc", [P, D])
        pz = ps("pz", [P, S])
        pt = ps("pt", [P, 1024])
        pm = ps("pm", [P, 1024])
        po = pm[:, 512:1024]

        chan_in = sem("chan_in")
        consts_in = sem("consts_in")
        cleared = sem("cleared")
        ident_set = sem("ident_set")
        ones_set = sem("ones_set")
        band_set = sem("band_set")
        keys_cleared = sem("keys_cleared")
        iota_set = sem("iota_set")
        x_in = sem("x_in")
        x_kept = sem("x_kept")
        w_in = [sem(f"w_in{i}") for i in range(W_SLOTS)]
        piece_done = sem("piece_done")
        norm1 = sem("norm1")
        h_ready = sem("h_ready")
        h_turned = sem("h_turned")
        hT_ready = sem("hT_ready")
        qk_sq = sem("qk_sq")
        qk_norm = sem("qk_norm")
        v_kept = sem("v_kept")
        qk_turned = sem("qk_turned")
        qkT_ready = sem("qkT_ready")
        xc_kept = sem("xc_kept")
        u_ready = sem("u_ready")
        cv_raw = sem("cv_raw")
        cv_sq = sem("cv_sq")
        cvT_ready = sem("cvT_ready")
        cv_ss = sem("cv_ss")
        cv_ss_kept = sem("cv_ss_kept")
        z_psum = sem("z_psum")
        z_masked = sem("z_masked")
        beta_ready = sem("beta_ready")
        a_ready = sem("a_ready")
        a_turned = sem("a_turned")
        aT_ready = sem("aT_ready")
        av_done = sem("av_done")
        sb_kept = sem("sb_kept")
        sb_turned = sem("sb_turned")
        sbT_ready = sem("sbT_ready")
        h2_ready = sem("h2_ready")
        h2_turned = sem("h2_turned")
        h2T_ready = sem("h2T_ready")
        pq_ready = sem("pq_ready")
        s_psum = sem("s_psum")
        s_ready = sem("s_ready")
        s_ranked = sem("s_ranked")
        gate_arg = sem("gate_arg")
        gate_exp = sem("gate_exp")
        idx_ready = sem("idx_ready")
        gates_ready = sem("gates_ready")
        idx_taken = sem("idx_taken")
        idx_slice = sem("idx_slice")
        h_mix_set = sem("h_mix_set")
        x_mix_set = sem("x_mix_set")
        u_in = [sem(f"u_in{i}") for i in range(U_SLOTS)]
        v_in = [sem(f"v_in{i}") for i in range(V_SLOTS)]
        dots_done = sem("dots_done")
        gelu_done = sem("gelu_done")
        wgt_ready = sem("wgt_ready")
        diag_ready = sem("diag_ready")
        group_done = sem("group_done")
        acc_free = sem("acc_free")
        x_mix_free = sem("x_mix_free")
        y_out = sem("y_out")
        passed = sem("passed")
        own_v = sem("own_v")

        def wait(eng, s, value):
            if not (isinstance(value, int) and value <= 0):
                eng.wait_ge(s, value)

        def apart(eng):
            eng.sem_inc(passed, 1)

        def at_once(b):
            return BLOCKS if isinstance(b, int) else 1

        def place(h, m):
            return 0 if m == 1 else (h % 2) * (m // 2) + h // 2

        def grid(ap, n):
            return ap.rearrange("p (a b) -> p a b", a=n)

        def spread(ap, n):
            return ap.unsqueeze(2).to_broadcast([ap.shape[0], ap.shape[1], n])

        block = ctx.enter_context(nc.Block())

        @block.sync
        def _(sp):
            def weights(b, pieces):
                for j in pieces:
                    wait(sp, piece_done, b * PIECES + j - W_SLOTS + 1)
                    sp.dma_start(w_ring[:, j % W_SLOTS, :], wstream[j]).then_inc(w_in[j % W_SLOTS], 16)

            def first(b):
                wait(sp, s_ranked, 4 * b)
                sp.dma_start(rb[:], x[bass.ds(b * P, P), :]).then_inc(x_in, 16)
                weights(b, range(W_SLOTS))

            def rest(b):
                weights(b, range(W_SLOTS, PIECES))

            def store(b):
                sp.wait_ge(acc_free, b + 2)
                sp.dma_start(out[bass.ds(b * P, P), :], x_mix[:]).then_inc(y_out, 16)
                sp.wait_ge(y_out, 16 * (b + 1))
                sp.sem_inc(x_mix_free, 1)

            sp.sem_inc(x_mix_free, 1)
            first(0)
            sp.dma_start(chan_sb[:], chan).then_inc(chan_in, 16)
            sp.dma_start(keysT[:], keys).then_inc(consts_in, 16)
            sp.dma_start(g2_all[:], norm2_g.to_broadcast([P, D])).then_inc(consts_in, 16)
            rest(0)
            first(1)
            with sp.Fori(1, BLOCKS - 1) as b:
                rest(b)
                first(b + 1)
                store(b - 1)
            rest(BLOCKS - 1)
            store(BLOCKS - 2)
            store(BLOCKS - 1)
            sp.wait_ge(y_out, 16 * BLOCKS)

        @block.gpsimd
        def _(pool):
            nc.gpsimd.memset(ident[:], 0.0).then_inc(cleared, 1)
            nc.gpsimd.iota(iota_i[:], [[1, TOPK]], base=0, channel_multiplier=0).then_inc(iota_set, 1)
            pool.wait_ge(cleared, 1)
            nc.gpsimd.affine_select(out=ident[:], in_=ident[:], compare_op=ALU.not_equal, fill=1.0, base=0,
                                    pattern=[[-1, P]], channel_multiplier=1).then_inc(ident_set, 1)
            nc.gpsimd.memset(ones[:], 1.0).then_inc(ones_set, 1)
            nc.gpsimd.memset(band[:], 0.0).then_inc(cleared, 1)
            pool.wait_ge(cleared, 2)
            nc.gpsimd.affine_select(out=band[:], in_=band[:], compare_op=ALU.is_gt, fill=MASKED,
                                    base=(BLOCKS - 1) * P, pattern=[[-1, S + 7 * P]],
                                    channel_multiplier=1).then_inc(band_set, 1)
            nc.gpsimd.memset(kT[:], 0.0).then_inc(keys_cleared, 1)
            nc.gpsimd.memset(vals_sb[:], 0.0).then_inc(keys_cleared, 1)

            def take(b, begin=0, end=PICKS):
                pool.wait_ge(idx_ready, 4 * b + end * 4 // PICKS)
                apart(pool)
                nc.gpsimd.tensor_copy(idx_mix[:, begin:end], idx_next[:, begin:end]).then_inc(idx_taken, 1)
                pool.wait_ge(idx_taken, b + 2 if end == PICKS else 1)
                apart(pool)

            def two_rounds(b, m):
                for r in range(2):
                    first = m * 2 * V_SLOTS + r * V_SLOTS
                    nc.gpsimd.tensor_copy(idx_now[:, r, :],
                                          idx_mix[:, bass.ds(first, V_SLOTS)]).then_inc(idx_slice, 1)
                    pool.wait_ge(idx_slice, (b * (PICKS // V_SLOTS)) + 2 * m + r + 1)
                    apart(pool)
                    for g in range(V_SLOTS // GROUP):
                        n = b * GROUPS + (2 * m + r) * (V_SLOTS // GROUP) + g
                        wait(pool, group_done, n + 1 - V_SLOTS // GROUP)
                        apart(pool)
                        for j in range(g * GROUP, (g + 1) * GROUP):
                            nc.gpsimd.indirect_dma_start(
                                out=v_ring[:, j, :], out_offset=None, in_=peer_v,
                                in_offset=bass.IndirectOffsetOnAxis(ap=idx_now[:, r, j:j + 1], axis=0),
                            ).then_inc(v_in[j], 16)
                        wait(pool, dots_done, n + 1 - U_SLOTS // GROUP)
                        apart(pool)
                        for j in range(g * GROUP, (g + 1) * GROUP):
                            nc.gpsimd.indirect_dma_start(
                                out=u_ring[:, j % U_SLOTS, :], out_offset=None, in_=peer_u,
                                in_offset=bass.IndirectOffsetOnAxis(ap=idx_now[:, r, j:j + 1], axis=0),
                            ).then_inc(u_in[j % U_SLOTS], 16)

            rounds = PICKS // (2 * V_SLOTS)
            take(0, 0, 2 * V_SLOTS)
            two_rounds(0, 0)
            take(0, 2 * V_SLOTS, PICKS)
            with pool.Fori(1, rounds) as m:
                two_rounds(0, m)
            with pool.Fori(1, BLOCKS) as b:
                take(b)
                with pool.Fori(0, rounds) as m:
                    two_rounds(b, m)

        @block.tensor
        def _(pe):
            def piece(b, j):
                pe.wait_ge(w_in[j % W_SLOTS], 16 * (b * (PIECES // W_SLOTS) + j // W_SLOTS + 1))
                return w_ring[:, j % W_SLOTS, :]

            def product(b, j):
                w = piece(b, j)
                if j < PIECE_XC:
                    o = (pm[:, 0:512], pm[:, 512:1024], pz[:, 0:512])[j // 4]
                    terms = [(o, hT[:, k, :], w[:, (k % 2) * 512:(k % 2 + 1) * 512], k == 0, k == KD - 1)
                             for k in (2 * (j % 4), 2 * (j % 4) + 1)]
                elif PIECE_OUT <= j < PIECE_PEER:
                    o, src = ((pz, cvT), (pm, sbT))[(j - PIECE_OUT) // 4]
                    half = (j % 4) // 2
                    terms = [(o[:, half * 512:(half + 1) * 512], src[:, c, :],
                              w[:, (c % 2) * 512:(c % 2 + 1) * 512], c == 0, c == CH - 1)
                             for c in (2 * (j % 2), 2 * (j % 2) + 1)]
                else:
                    q = (j - PIECE_PEER) // 4
                    bank = 0 if j < PIECE_OUT else (q % 2) * 512
                    o = pm[:, bank + (j % 4) * P:bank + (j % 4 + 1) * P]
                    terms = [(o, w[:, k * P:(k + 1) * P], hT[:, k, :], k == 0, k == KD - 1) for k in range(KD)]
                for o, left, right, start, stop in terms:
                    mm = nc.tensor.matmul(o, left, right, start=start, stop=stop)
                mm.then_inc(piece_done, 1)

            def turn(dst, src, tiles):
                for t in range(tiles):
                    mm = nc.tensor.transpose(dst[:, t * P:(t + 1) * P], src[:, t * P:(t + 1) * P], ident[:])
                return mm

            def scores(b, i):
                m = at_once(b)
                n = S // m
                if i == 0:
                    pe.wait_ge(v_kept, b + 1)
                    pe.wait_ge(qkT_ready, 2 * b + 2)
                wait(pe, z_masked, b * HEADS + i * m)
                for h in range(i * m, (i + 1) * m):
                    r, here = DH * (h % 2), place(h, m) * n
                    for o in range(0, n, 512):
                        w = min(512, n)
                        mm = nc.tensor.matmul(pz[:, here + o:here + o + w], qT[r:r + DH, h // 2, :],
                                              kT[r:r + DH, h // 2, o:o + w], start=True, stop=True)
                mm.then_inc(z_psum, m)

            def values(b, i):
                m = at_once(b)
                tiles = BLOCKS // m
                pe.wait_ge(aT_ready, b * HEADS + (i + 1) * m)
                for h in range(i * m, (i + 1) * m):
                    for t in range(tiles):
                        here = (place(h, m) * tiles + t) * P
                        mm = nc.tensor.matmul(po[:, h * DH:(h + 1) * DH], rd[:, here:here + P],
                                              vals_sb[:, t, h * DH:(h + 1) * DH],
                                              start=(t == 0), stop=(t == tiles - 1))
                mm.then_inc(av_done, m)

            def peer_scores(b, q):
                pe.wait_ge(pq_ready, 4 * b + q + 1)
                if q >= 2:
                    pe.wait_ge(s_ready, 4 * b + q - 1)
                o = (q % 2) * 512
                for c in range(4):
                    mm = nc.tensor.matmul(pz[:, o + c * P:o + (c + 1) * P], rd[:, o + c * P:o + (c + 1) * P],
                                          keysT[:, (c % 2) * NKEYS:(c % 2 + 1) * NKEYS],
                                          start=True, stop=True)
                mm.then_inc(s_psum, 1)

            def early(b, t):
                if t == S_QK + 1:
                    pe.wait_ge(qk_norm, 2 * b + 2)
                    turn(pt, rb, 8).then_inc(qk_turned, 1)
                m = at_once(b)
                if S_HEAD < t <= S_HEAD + HEADS // m:
                    i = t - S_HEAD - 1
                    pe.wait_ge(a_ready, b * HEADS + (i + 1) * m)
                    if i >= 1:
                        pe.wait_ge(aT_ready, b * HEADS + i * m)
                    turn(pt, rb, BLOCKS).then_inc(a_turned, m)

            def late(b, t):
                if t == S_NORM1 + 1:
                    pe.wait_ge(h_ready, b + 1)
                    wait(pe, h2T_ready, b)
                    turn(pt, ra, KD).then_inc(h_turned, 1)
                steps = HEADS // at_once(b)
                if S_HEAD < t <= S_HEAD + steps:
                    values(b, t - S_HEAD - 1)
                if S_HEAD - 1 <= t < S_HEAD - 1 + steps:
                    scores(b, t - S_HEAD + 1)
                if t == S_CONV + 6:
                    pe.wait_ge(cv_sq, b + 1)
                    for c in range(CH):
                        mm = nc.tensor.matmul(pm[:, 0:1], h_next[:, 512 + c * P:512 + (c + 1) * P], ones[:],
                                              start=(c == 0), stop=(c == CH - 1))
                    mm.then_inc(cv_ss, 1)
                if t == S_SB:
                    pe.wait_ge(sb_kept, b + 1)
                    turn(pt, rd, CH).then_inc(sb_turned, 1)
                if t == S_NORM2:
                    pe.wait_ge(h2_ready, b + 1)
                    turn(pt, h_next, KD).then_inc(h2_turned, 1)
                if t == S_PROJ:
                    pe.wait_ge(hT_ready, b + 1)
                    wait(pe, s_ready, b * 4)
                if t == S_CONV + 2:
                    pe.wait_ge(xc_kept, b + 1)
                if t == S_CONV + 4:
                    pe.wait_ge(u_ready, b + 1)
                if t == S_CONV_OUT:
                    pe.wait_ge(cvT_ready, b + 1)
                    pe.wait_ge(z_masked, (b + 1) * HEADS)
                if t == S_OUT:
                    pe.wait_ge(sbT_ready, b + 1)
                    pe.wait_ge(cv_ss_kept, b + 1)
                if t == S_PEER:
                    pe.wait_ge(h2T_ready, b + 1)
                for j in range(*PIECES_AT.get(t, (0, 0))):
                    if j in (PIECE_PEER + 8, PIECE_PEER + 12):
                        pe.wait_ge(pq_ready, 4 * b + (j - PIECE_PEER) // 4 - 1)
                    product(b, j)
                if S_PEER + 1 <= t < S_PEER + 5:
                    peer_scores(b, t - S_PEER - 1)

            def mix(b, n):
                pe.wait_ge(diag_ready, b * GROUPS + n + 1)
                if n == 0:
                    pe.wait_ge(acc_free, b + 1)
                for j in range(GROUP):
                    k = n * GROUP + j
                    pe.wait_ge(v_in[k % V_SLOTS], 16 * (b * (PICKS // V_SLOTS) + k // V_SLOTS + 1))
                    for half in range(2):
                        mm = nc.tensor.matmul(acc[:, half * 512:(half + 1) * 512], diag[:, n % 2, j, :],
                                              v_ring[:, k % V_SLOTS, half * 512:(half + 1) * 512],
                                              start=(k == 0), stop=(k == PICKS - 1))
                mm.then_inc(group_done, 1)

            pe.wait_ge(ident_set, 1)
            pe.wait_ge(ones_set, 1)
            for t in range(S_LAST + 1):
                if t == S_PEER:
                    pe.wait_ge(consts_in, 32)
                early(0, t)
                late(0, t)
            with pe.Fori(1, BLOCKS) as b:
                for t in range(GROUPS):
                    early(b, t)
                    if t >= 1:
                        mix(b - 1, t - 1)
                    late(b, t)
                mix(b - 1, GROUPS - 1)
            for n in range(GROUPS):
                mix(BLOCKS - 1, n)

        @block.scalar
        def _(act):
            copy = ACT.Copy

            def front(b, t):
                if t == S_NORM1 + 1:
                    act.wait_ge(norm1, b + 1)
                    nc.scalar.activation(ra[:, 0:D], rb[:], copy, scale=inv1[:]).then_inc(h_ready, 1)
                if t == S_NORM1 + 2:
                    wait(act, x_mix_set, b)
                    nc.scalar.activation(x_next[:], rb[:], copy).then_inc(x_kept, 1)
                if t == S_QK:
                    act.wait_ge(piece_done, b * PIECES + PIECE_K + 4)
                    for i in range(2):
                        nc.scalar.activation(rc[:, i * 512:(i + 1) * 512], pm[:, i * 512:(i + 1) * 512],
                                             ACT.Square).then_inc(qk_sq, 1)
                if t == S_QK + 1:
                    if isinstance(b, int):
                        act.wait_ge(keys_cleared, 2)
                    act.wait_ge(qk_turned, b + 1)
                    nc.scalar.activation(qT[:], grid(pt[:, 0:512], CH), copy,
                                         scale=chan_sb[:, C_GQ:C_GQ + 1]).then_inc(qkT_ready, 1)
                    nc.scalar.activation(kT[:, :, bass.ds(b * P, P)], grid(pt[:, 512:1024], CH), copy,
                                         scale=chan_sb[:, C_GK:C_GK + 1]).then_inc(qkT_ready, 1)
                    act.wait_ge(piece_done, b * PIECES + PIECE_V + 4)
                    nc.scalar.activation(vals_sb[:, bass.ds(b, 1), :], pz[:, 0:512].unsqueeze(1),
                                         copy).then_inc(v_kept, 1)
                if t == S_CONV + 2:
                    act.wait_ge(piece_done, b * PIECES + PIECE_XC + 4)
                    nc.scalar.activation(h_next[:, 0:512], pm[:, 0:512], copy).then_inc(xc_kept, 1)
                if t == S_CONV + 6:
                    act.wait_ge(cv_raw, b + 1)
                    nc.scalar.activation(h_next[:, 512:1024], h_next[:, 0:512], ACT.Square).then_inc(cv_sq, 1)
                m = at_once(b)
                if S_HEAD < t <= S_HEAD + HEADS // m:
                    i = t - S_HEAD - 1
                    act.wait_ge(a_turned, b * HEADS + (i + 1) * m)
                    wait(act, av_done, b * HEADS + i * m)
                    if i == 0:
                        wait(act, s_psum, 4 * b)
                    nc.scalar.activation(rd[:], pt[:], copy).then_inc(aT_ready, m)
                if S_HEAD <= t < S_HEAD + HEADS // m:
                    i = t - S_HEAD
                    act.wait_ge(z_masked, b * HEADS + (i + 1) * m)
                    nc.scalar.activation(rb[:], ra[:], ACT.Sigmoid, scale=SCALE)
                    nc.scalar.activation(rc[:], ra[:], ACT.Sigmoid, scale=-SCALE).then_inc(beta_ready, m)
                if t == S_SB:
                    act.wait_ge(av_done, (b + 1) * HEADS)
                    nc.scalar.activation(rd[:, 0:512], po, copy).then_inc(sb_kept, 1)
                if t == S_NORM2 + 1:
                    act.wait_ge(h2_turned, b + 1)
                    nc.scalar.activation(hT[:], grid(pt[:], KD), copy).then_inc(h2T_ready, 1)
                if S_RANK <= t < S_RANK + 4:
                    q, o = t - S_RANK, ((t - S_RANK) % 2) * 512
                    act.wait_ge(s_psum, 4 * b + q + 1)
                    if q >= 2:
                        act.wait_ge(s_ranked, 4 * b + q - 1)
                    nc.scalar.activation(rb[:, o:o + 512], pz[:, o:o + 512], copy).then_inc(s_ready, 1)
                if S_PEER + 1 <= t < S_PEER + 5:
                    q, o = t - S_PEER - 1, ((t - S_PEER - 1) % 2) * 512
                    act.wait_ge(piece_done, b * PIECES + PIECE_PEER + 4 * (q + 1))
                    if q == 0:
                        act.wait_ge(sb_turned, b + 1)
                    nc.scalar.activation(rd[:, o:o + 512], pm[:, o:o + 512], copy).then_inc(pq_ready, 1)
                if t == S_LAST - 1:
                    act.wait_ge(gate_arg, b + 1)
                    nc.scalar.activation(gate_e[:], gate_e[:], ACT.Exp).then_inc(gate_exp, 1)

            def diagonals(b, n):
                act.wait_ge(wgt_ready, b * GROUPS + n + 1)
                if n == 0:
                    act.wait_ge(acc_free, b + 1)
                else:
                    wait(act, group_done, b * GROUPS + n - 1)
                for j in range(GROUP):
                    a = nc.scalar.activation(diag[:, n % 2, j, :], ident[:], copy, scale=wgt[:, n % 2, j:j + 1])
                a.then_inc(diag_ready, 1)

            def gelu(b, n):
                act.wait_ge(dots_done, b * GROUPS + n + 1)
                nc.scalar.activation(acts[:, n % 2, :], dots[:, n % 2, :], ACT.Gelu).then_inc(gelu_done, 1)

            def take_h(b):
                act.wait_ge(h2_turned, b + 1)
                nc.scalar.activation(h_mix[:], h_next[:], copy).then_inc(h_mix_set, 1)

            def take_gates(b):
                act.wait_ge(gates_ready, b + 1)
                nc.scalar.activation(gate_mix[:], gate_next[:].rearrange("p h k -> p (h k)"),
                                     copy).then_inc(h_mix_set, 1)

            def take_residual(b):
                act.wait_ge(x_mix_free, b + 1)
                nc.scalar.activation(x_mix[:], x_next[:], copy).then_inc(x_mix_set, 1)

            act.wait_ge(chan_in, 16)
            act.wait_ge(ident_set, 1)
            for t in range(S_LAST + 1):
                front(0, t)
                if t == S_PEER + 1:
                    take_h(0)
            take_gates(0)
            with act.Fori(1, BLOCKS) as b:
                for t in range(GROUPS):
                    if t >= 1:
                        diagonals(b - 1, t - 1)
                    front(b, t)
                    gelu(b - 1, t)
                    if t == 1:
                        take_residual(b - 1)
                take_h(b)
                diagonals(b - 1, GROUPS - 1)
                take_gates(b)
            for n in range(GROUPS):
                if n >= 1:
                    diagonals(BLOCKS - 1, n - 1)
                gelu(BLOCKS - 1, n)
                if n == 1:
                    take_residual(BLOCKS - 1)
            diagonals(BLOCKS - 1, GROUPS - 1)

        @block.vector
        def _(dve):
            V = nc.vector
            count = {"here": 0, "front": 0}

            def step(ins):
                ins.then_inc(own_v, 1)
                count["here"] += 1

            def settle(b):
                dve.wait_ge(own_v, b * count["front"] + count["here"])

            def inverse_root(b, o, sums, n, scale, done=None):
                a, t = rs_a[:, 0:n], rs_t[:, 0:n]
                step(V.tensor_scalar(a, sums, scale, EPS, ALU.mult, ALU.add))
                settle(b)
                step(V.tensor_scalar(o.bitcast(I32), a.bitcast(I32), 1, None, ALU.logical_shift_right))
                settle(b)
                step(V.tensor_scalar(o.bitcast(I32), o.bitcast(I32), -1.0, MAGIC, ALU.mult, ALU.add))
                settle(b)
                for i in range(4):
                    step(V.tensor_tensor(t, o, o, ALU.mult))
                    settle(b)
                    step(V.scalar_tensor_tensor(t, t, -0.5, a, ALU.mult, ALU.mult))
                    settle(b)
                    last = V.scalar_tensor_tensor(o, t, 1.5, o, ALU.add, ALU.mult)
                    if i == 3 and done is not None:
                        last.then_inc(done, 1)
                    else:
                        step(last)
                        settle(b)

            def square_sum(b, src, junk, o):
                step(V.tensor_tensor_reduce(junk, src, src, 1.0, 0.0, ALU.mult, ALU.add, o))

            def mask(b, i):
                m = at_once(b)
                n = S // m
                dve.wait_ge(z_psum, b * HEADS + (i + 1) * m)
                if i >= 1:
                    dve.wait_ge(a_ready, b * HEADS + i * m)
                apart(dve)
                open_to = band[:, bass.ds((BLOCKS - 1 - b) * P, n)]
                if m > 1:
                    open_to = open_to.unsqueeze(1).to_broadcast([P, m, n])
                    V.tensor_tensor(grid(ra[:], m), grid(pz[:], m), open_to, ALU.add).then_inc(z_masked, m)
                else:
                    V.tensor_tensor(ra[:], pz[:], open_to, ALU.add).then_inc(z_masked, 1)

            def stick(b, i):
                m = at_once(b)
                n = S // m
                dve.wait_ge(beta_ready, b * HEADS + (i + 1) * m)
                for j in range(m):
                    here = slice(j * n, (j + 1) * n)
                    step(V.tensor_tensor_scan(ra[:, here][:, ::-1], rc[:, here][:, ::-1], rc[:, here][:, ::-1], 1.0,
                                              ALU.mult, ALU.bypass))
                settle(b)
                a, e = (ap[:] if m == 1 else grid(ap[:], m) for ap in (rb, ra))
                V.tensor_tensor(a[..., 0:n - 1], a[..., 0:n - 1], e[..., 1:n], ALU.mult).then_inc(a_ready, m)

            def rank(b, q):
                dve.wait_ge(s_ready, 4 * b + q + 1)
                o = (q % 2) * 512
                apart(dve)
                row = lambda r, c: r[:, o + c * NKEYS:o + (c + 1) * NKEYS]
                for c in range(4):
                    step(V.max(top_v[:, 4 * q + c, 0:8], row(rb, c)))
                settle(b)
                apart(dve)
                for c in range(4):
                    step(V.max_index(top_i[:, 4 * q + c, 0:8], top_v[:, 4 * q + c, 0:8], row(rb, c)))
                for c in range(4):
                    step(V.match_replace(row(rc, c), top_v[:, 4 * q + c, 0:8], row(rb, c), TAKEN))
                settle(b)
                apart(dve)
                for c in range(4):
                    step(V.max(top_v[:, 4 * q + c, 8:16], row(rc, c)))
                settle(b)
                apart(dve)
                for c in range(4):
                    i = V.max_index(top_i[:, 4 * q + c, 8:16], top_v[:, 4 * q + c, 8:16], row(rc, c))
                i.then_inc(s_ranked, 1)

            def combine(b, q, ranked):
                dve.wait_ge(s_ranked, 4 * b + ranked)
                first = top_v[:, 4 * q:4 * q + 4:2, :].unsqueeze(3).to_broadcast([P, 2, TOPK, TOPK])
                second = top_v[:, 4 * q + 1:4 * q + 4:2, :].unsqueeze(2).to_broadcast([P, 2, TOPK, TOPK])
                step(V.tensor_tensor(rc[:, 0:512].rearrange("p (h i j) -> p h i j", h=2, i=TOPK), first, second,
                                     ALU.add))
                settle(b)
                apart(dve)
                row = lambda r, c: r[:, c * 256:(c + 1) * 256]
                heads = [(2 * q + c, c) for c in range(2)]
                for h, c in heads:
                    step(V.max(sum_v[:, h, 0:8], row(rc, c)))
                settle(b)
                apart(dve)
                for h, c in heads:
                    step(V.max_index(sum_p[:, h, 0:8], sum_v[:, h, 0:8], row(rc, c)))
                for h, c in heads:
                    step(V.match_replace(row(ra, c), sum_v[:, h, 0:8], row(rc, c), TAKEN))
                settle(b)
                apart(dve)
                for h, c in heads:
                    step(V.max(sum_v[:, h, 8:16], row(ra, c)))
                settle(b)
                apart(dve)
                for h, c in heads:
                    step(V.max_index(sum_p[:, h, 8:16], sum_v[:, h, 8:16], row(ra, c)))
                settle(b)

            def look_up(b, q):
                k0, n = 2 * q * TOPK, 2 * TOPK
                flat = sum_p[:, 2 * q:2 * q + 2, :].rearrange("p h k -> p (h k)")
                step(V.tensor_scalar(pos[:, 0, k0:k0 + n], flat, 4, None, ALU.logical_shift_right))
                step(V.tensor_scalar(pos[:, 1, k0:k0 + n], flat, 15, None, ALU.bitwise_and))
                step(V.tensor_copy(top_f[:, 4 * q:4 * q + 4, :], top_i[:, 4 * q:4 * q + 4, :]))
                settle(b)
                step(V.tensor_copy(pos_f[:, :, k0:k0 + n], pos[:, :, k0:k0 + n]))
                settle(b)
                hot = [ra[:, i * 512:(i + 1) * 512] for i in range(2)]
                for i in range(2):
                    step(V.tensor_tensor(grid(hot[i], n), iota_f[:].unsqueeze(1).to_broadcast([P, n, TOPK]),
                                         spread(pos_f[:, i, k0:k0 + n], TOPK), ALU.is_equal))
                settle(b)
                for i in range(2):
                    h = hot[i].rearrange("p (h k a) -> p h k a", h=2, a=TOPK)
                    step(V.tensor_tensor(h, h, top_f[:, 4 * q + i:4 * q + 4:2, :].unsqueeze(2)
                                         .to_broadcast([P, 2, TOPK, TOPK]), ALU.mult))
                settle(b)
                for i in range(2):
                    step(V.tensor_reduce(sel[:, i, k0:k0 + n], grid(hot[i], n), AX_X, ALU.add))
                settle(b)
                if not isinstance(b, int):
                    dve.wait_ge(idx_taken, b + 1)
                V.scalar_tensor_tensor(idx_next[:, k0:k0 + n], sel[:, 0, k0:k0 + n], float(NKEYS),
                                       sel[:, 1, k0:k0 + n], ALU.mult, ALU.add).then_inc(idx_ready, 1)

            def early(b, t):
                if t == S_NORM1:
                    dve.wait_ge(x_in, 16 * (b + 1))
                    square_sum(b, rb[:], ra[:, 0:D], ss[:, 0:1])
                    settle(b)
                    inverse_root(b, inv1[:], ss[:, 0:1], 1, 1.0 / D, done=norm1)
                if t == S_PROJ:
                    dve.wait_ge(h_turned, b + 1)
                    V.tensor_tensor(hT[:], grid(pt[:], KD), spread(chan_sb[:, C_G1:C_G1 + KD], P),
                                    ALU.mult).then_inc(hT_ready, 1)
                if S_HEAD <= t < S_HEAD + HEADS // at_once(b):
                    mask(b, t - S_HEAD)
                if t == S_CONV + 4:
                    step(V.tensor_copy(uT[:, :, 0:2], uT[:, :, P:P + 2]))
                    settle(b)
                    dve.wait_ge(xc_kept, b + 1)
                    dve.wait_ge(piece_done, b * PIECES + PIECE_C + 4)
                    V.tensor_tensor(uT[:, :, 2:P + 2], grid(pm[:, 0:512], CH), grid(h_next[:, 0:512], CH),
                                    ALU.mult).then_inc(u_ready, 1)
                if t == S_CONV + 6:
                    dve.wait_ge(piece_done, b * PIECES + PIECE_B + 4)
                    V.tensor_tensor(grid(h_next[:, 0:512], CH), grid(pm[:, 0:512], CH),
                                    grid(h_next[:, 512:1024], CH), ALU.mult).then_inc(cv_raw, 1)
                    dve.wait_ge(cv_raw, b + 1)
                    wait(dve, idx_ready, 4 * b)
                    V.tensor_tensor(cvT[:], grid(h_next[:, 0:512], CH), spread(chan_sb[:, C_GCV:C_GCV + CH], P),
                                    ALU.mult).then_inc(cvT_ready, 1)
                if t == S_CONV + 7:
                    dve.wait_ge(cv_ss, b + 1)
                    V.tensor_copy(ss2[:, 1:2], pm[:, 0:1]).then_inc(cv_ss_kept, 1)
                if t == S_OUT:
                    dve.wait_ge(sb_turned, b + 1)
                    V.tensor_tensor(sbT[:], grid(pt[:, 0:512], CH), spread(chan_sb[:, C_GSB:C_GSB + CH], P),
                                    ALU.mult).then_inc(sbT_ready, 1)
                if t == S_NORM2:
                    dve.wait_ge(x_kept, b + 1)
                    for i, o in ((1, pz), (0, pm)):
                        dve.wait_ge(piece_done, b * PIECES + PIECE_OUT + 8 - 4 * i)
                        step(V.scalar_tensor_tensor(x_next[:], o[:], inv2[:, i:i + 1], x_next[:], ALU.mult, ALU.add))
                        settle(b)
                    square_sum(b, x_next[:], ra[:, 0:D], ss[:, 0:1])
                    settle(b)
                    inverse_root(b, invh[:], ss[:, 0:1], 1, 1.0 / D)
                    V.scalar_tensor_tensor(h_next[:], x_next[:], invh[:], g2_all[:], ALU.mult,
                                           ALU.mult).then_inc(h2_ready, 1)
                join = S_JOIN_FIRST if isinstance(b, int) else S_JOIN
                if t in join:
                    combine(b, join[t], min(4, t - S_RANK))
                    if join[t] == 3:
                        V.tensor_tensor(gate_e[:], sum_v[:], sum_v[:, :, 0:1].to_broadcast([P, PH, TOPK]),
                                        ALU.subtract).then_inc(gate_arg, 1)

            def late(b, t):
                if t == S_QK:
                    dve.wait_ge(qk_sq, 2 * (b + 1))
                    step(V.tensor_reduce(ss[:], grid(rc[:], 2 * HEADS), AX_X, ALU.add))
                    settle(b)
                    inverse_root(b, invqk[:], ss[:], 2 * HEADS, 1.0 / DH)
                    dve.wait_ge(x_kept, b + 1)
                    for i in range(2):
                        V.tensor_tensor(grid(rb[:, i * 512:(i + 1) * 512], HEADS),
                                        grid(pm[:, i * 512:(i + 1) * 512], HEADS),
                                        spread(invqk[:, i * HEADS:(i + 1) * HEADS], DH),
                                        ALU.mult).then_inc(qk_norm, 1)
                if S_HEAD <= t < S_HEAD + HEADS // at_once(b):
                    stick(b, t - S_HEAD)
                if t == S_CONV + 4:
                    y = grid(h_next[:, 512:1024], CH)
                    tap = lambda w, c: chan_sb[:, C_CONV + w * CH + c:C_CONV + w * CH + c + 1]
                    dve.wait_ge(u_ready, b + 1)
                    for c in range(CH):
                        step(V.tensor_scalar(y[:, c, :], uT[:, c, 0:P], tap(0, c), None, ALU.mult))
                    for w in (1, 2):
                        settle(b)
                        for c in range(CH):
                            step(V.scalar_tensor_tensor(y[:, c, :], uT[:, c, w:w + P], tap(w, c), y[:, c, :],
                                                        ALU.mult, ALU.add))
                    settle(b)
                if t == S_SB:
                    dve.wait_ge(sb_kept, b + 1)
                    square_sum(b, rd[:, 0:512], rb[:, 0:512], ss2[:, 0:1])
                    settle(b)
                    inverse_root(b, inv2[:], ss2[:], 2, 1.0 / DSB)
                if S_RANK <= t < S_RANK + 4:
                    rank(b, t - S_RANK)
                look = S_LOOK_FIRST if isinstance(b, int) else S_LOOK
                if t in look:
                    look_up(b, look[t])
                if t == S_LAST:
                    dve.wait_ge(gate_exp, b + 1)
                    step(V.tensor_reduce(den[:], gate_e[:], AX_X, ALU.add))
                    settle(b)
                    step(V.reciprocal(rden[:], den[:]))
                    settle(b)
                    wait(dve, h_mix_set, 2 * b)
                    V.tensor_tensor(gate_next[:], gate_e[:], spread(rden[:], TOPK),
                                    ALU.mult).then_inc(gates_ready, 1)

            def weights(b, n):
                dve.wait_ge(gelu_done, b * GROUPS + n + 1)
                if n == 0:
                    dve.wait_ge(h_mix_set, 2 * b + 2)
                V.tensor_tensor(wgt[:, n % 2, :], acts[:, n % 2, :], gate_mix[:, n * GROUP:(n + 1) * GROUP],
                                ALU.mult).then_inc(wgt_ready, 1)

            def dot(b, n):
                for j in range(GROUP):
                    k = n * GROUP + j
                    dve.wait_ge(u_in[k % U_SLOTS], 16 * (b * (PICKS // U_SLOTS) + k // U_SLOTS + 1))
                    u = u_ring[:, k % U_SLOTS, :]
                    d = V.tensor_tensor_reduce(u, u, h_mix[:], 1.0, 0.0, ALU.mult, ALU.add,
                                               dots[:, n % 2, j:j + 1])
                d.then_inc(dots_done, 1)

            def finish(b):
                dve.wait_ge(group_done, (b + 1) * GROUPS)
                dve.wait_ge(x_mix_set, b + 1)
                V.tensor_tensor(x_mix[:], acc[:], x_mix[:], ALU.add).then_inc(acc_free, 1)

            dve.sem_inc(acc_free, 1)
            step(V.memset(uT[:], 0.0))
            dve.wait_ge(iota_set, 1)
            step(V.tensor_copy(iota_f[:], iota_i[:]))
            settle(0)
            set_up = count["here"]
            for t in range(S_LAST + 1):
                if t == S_PROJ:
                    dve.wait_ge(chan_in, 16)
                if t == S_HEAD:
                    dve.wait_ge(band_set, 1)
                if t == S_NORM2:
                    dve.wait_ge(consts_in, 32)
                early(0, t)
                if t in S_DOTS_FIRST:
                    dve.wait_ge(h_mix_set, 1)
                    dot(0, S_DOTS_FIRST[t])
                late(0, t)
            count["front"] = count["here"] - set_up
            with dve.Fori(1, BLOCKS) as b:
                count["here"] = set_up
                for t in range(GROUPS):
                    if t >= 1:
                        weights(b - 1, t - 1)
                    early(b, t)
                    if t >= 2:
                        dot(b - 1, t)
                    late(b, t)
                weights(b - 1, GROUPS - 1)
                dve.wait_ge(h_mix_set, 2 * b + 1)
                dot(b, 0)
                dot(b, 1)
                finish(b - 1)
            for n in range(1, GROUPS):
                weights(BLOCKS - 1, n - 1)
                if n >= 2:
                    dot(BLOCKS - 1, n)
            weights(BLOCKS - 1, GROUPS - 1)
            finish(BLOCKS - 1)


def kernel(x, norm1_g, w_in, q_norm_g, k_norm_g, conv_w, sb_out_g, conv_out_g, w_out, norm2_g, peer_w_q,
           peer_sub_keys, peer_u, peer_v):
    import numpy as np
    import concourse.bacc as bacc
    from concourse.bass_utils import run_bass_kernel_spmd

    def by_rows(w):
        n = w.shape[1] // 512
        w = w.reshape(4, 2, P, n, 512).transpose(3, 0, 2, 1, 4)
        return w.reshape(4 * n, P, 1024)

    def by_columns(w):
        n = w.shape[1] // P
        return w.reshape(KD, P, n, P).transpose(2, 1, 0, 3).reshape(n, P, 1024)

    def conv_first(pieces):
        return pieces.reshape(2, 2, 2, P, 1024)[:, ::-1].transpose(1, 0, 2, 3, 4).reshape(8, P, 1024)

    a = {k: np.asarray(v)[0] for k, v in dict(
        x=x, norm1_g=norm1_g, w_in=w_in, q_norm_g=q_norm_g, k_norm_g=k_norm_g, conv_w=conv_w, sb_out_g=sb_out_g,
        conv_out_g=conv_out_g, w_out=w_out, peer_w_q=peer_w_q, peer_sub_keys=peer_sub_keys, peer_u=peer_u,
        peer_v=peer_v).items()}
    part = [a["w_in"][:, i * DSB:(i + 1) * DSB] for i in range(6)]
    wstream = np.concatenate([by_rows(part[0]), by_rows(part[1]), by_rows(part[2]), by_columns(part[3]),
                              by_columns(part[5]), by_columns(part[4]), conv_first(by_rows(a["w_out"])),
                              by_columns(a["peer_w_q"])])
    chan = np.concatenate([
        a["norm1_g"].reshape(KD, P).T, a["conv_w"].reshape(3, CH, P).transpose(2, 0, 1).reshape(P, 3 * CH),
        a["conv_out_g"].reshape(CH, P).T, a["sb_out_g"].reshape(CH, P).T,
        np.concatenate([a["q_norm_g"]] * 2)[:, None], np.concatenate([a["k_norm_g"]] * 2)[:, None]], axis=1)
    arrays = {
        "x_in_dram": a["x"], "wstream": wstream, "chan": chan,
        "keys": a["peer_sub_keys"].transpose(2, 0, 1).reshape(P, 2 * NKEYS), "norm2": np.asarray(norm2_g),
        "table_u": a["peer_u"], "table_v": a["peer_v"],
    }
    arrays = {k: np.ascontiguousarray(v) for k, v in arrays.items()}
    nc = bacc.Bacc("TRN2", target_bir_lowering=False, num_devices=1)
    ins = [nc.dram_tensor(k, v.shape, F32, kind="ExternalInput").ap() for k, v in arrays.items()]
    out = nc.dram_tensor("y_out_dram", (S, D), F32, kind="ExternalOutput").ap()
    build(nc, *ins, out)
    r = run_bass_kernel_spmd(nc, [arrays], core_ids=[0])
    return r.results[0]["y_out_dram"].reshape(1, S, D)
```
